# Optimizing a Trainium2 kernel written in Bass

```python
import math, functools
import jax, jax.numpy as jnp
from jax import lax
import numpy as np

D_MODEL = 1024
BATCH = 1
SEQ = 1024
DEPTH = 2
DEC_BATCH = 8
DEC_SEQ = 4
PAST_LEN = 1024
PAGE_SIZE = 128

N_A_LAYERS = DEPTH // 2
N_C_LAYERS = DEPTH - N_A_LAYERS
A_HEADS = 4
A_QK_DIM = 64
A_V_DIM = 2 * A_QK_DIM
A_WIDTH = A_HEADS * A_V_DIM
ROPE_DIM = A_QK_DIM // 4
ROPE_THETA = 500000.0
B_WIDTH = D_MODEL - A_WIDTH
CONV_WIDTH = 31
IN_AB = 3 * A_WIDTH + 2 * B_WIDTH
C_HEAD = 64
C_HEADS = D_MODEL // C_HEAD
LORA_DECAY = 64
LORA_A = 64
LORA_MV = 32
LORA_GATE = 160
D_FF = ((8 * D_MODEL + 3 * 256 - 1) // (3 * 256)) * 256
Q_BLOCK = 128
NORM_EPS = 1e-6
SUBLN_EPS = 1e-5
LN_EPS = 1e-5
GN_EPS = 64e-5

kernel_name = 'diffattn_conformer_rwkv7_hybrid_step'

F32 = jnp.float32

def rmsnorm(x, g, eps=NORM_EPS):
    xf = x.astype(F32)
    y = xf * lax.rsqrt(jnp.mean(xf * xf, axis=-1, keepdims=True) + eps)
    return (y * g.astype(F32)).astype(x.dtype)

def layernorm(x, g, b, eps=LN_EPS):
    xf = x.astype(F32)
    mu = jnp.mean(xf, axis=-1, keepdims=True)
    var = jnp.mean(jnp.square(xf - mu), axis=-1, keepdims=True)
    y = (xf - mu) * lax.rsqrt(var + eps)
    return (y * g.astype(F32) + b.astype(F32)).astype(x.dtype)

def rope_partial(x, pos):
    half = ROPE_DIM // 2
    inv = 1.0 / (ROPE_THETA ** (jnp.arange(0, ROPE_DIM, 2, dtype=F32) / ROPE_DIM))
    ang = pos.astype(F32)[:, None] * inv[None, :]
    cos = jnp.cos(ang)[:, None, None, :]
    sin = jnp.sin(ang)[:, None, None, :]
    xf = x.astype(F32)
    x1 = xf[..., :half]
    x2 = xf[..., half:ROPE_DIM]
    out = jnp.concatenate([x1 * cos - x2 * sin, x2 * cos + x1 * sin, xf[..., ROPE_DIM:]], axis=-1)
    return out.astype(x.dtype)

def diff_lambda(lam_p, layer):
    lf = lam_p.astype(F32)
    lam_init = 0.8 - 0.6 * math.exp(-0.3 * layer)
    lam = jnp.exp(jnp.sum(lf[0] * lf[1])) - jnp.exp(jnp.sum(lf[2] * lf[3])) + lam_init
    return lam, lam_init

def diff_attn_prompt(q, k, v, lam):
    B, T = q.shape[:2]
    nb = T // Q_BLOCK
    scale = A_QK_DIM ** -0.5
    qb = jnp.swapaxes(q.reshape(B, nb, Q_BLOCK, A_HEADS, 2, A_QK_DIM), 0, 1)
    kpos = jnp.arange(T)

    def block(args):
        qi, bi = args
        s = jnp.einsum('bqhmd,bkhmd->bhmqk', qi, k).astype(F32) * scale
        qpos = bi * Q_BLOCK + jnp.arange(Q_BLOCK)
        s = jnp.where(kpos[None, :] <= qpos[:, None], s, -jnp.inf)
        pr = jax.nn.softmax(s, axis=-1)
        att = pr[:, :, 0] - lam * pr[:, :, 1]
        return jnp.einsum('bhqk,bkhe->bqhe', att.astype(v.dtype), v)

    out = lax.map(block, (qb, jnp.arange(nb)))
    return jnp.swapaxes(out, 0, 1).reshape(B, T, A_HEADS, A_V_DIM)

def diff_attn_sample(q, k_new, v_new, k_past, v_past, lam):
    Tn = q.shape[1]
    P = k_past.shape[1]
    scale = A_QK_DIM ** -0.5
    s_past = jnp.einsum('bqhmd,bkhmd->bhmqk', q, k_past).astype(F32) * scale
    s_new = jnp.einsum('bqhmd,bkhmd->bhmqk', q, k_new).astype(F32) * scale
    causal = jnp.arange(Tn)[None, :] <= jnp.arange(Tn)[:, None]
    s_new = jnp.where(causal, s_new, -jnp.inf)
    pr = jax.nn.softmax(jnp.concatenate([s_past, s_new], axis=-1), axis=-1)
    att = (pr[:, :, 0] - lam * pr[:, :, 1]).astype(v_new.dtype)
    return (jnp.einsum('bhqk,bkhe->bqhe', att[..., :P], v_past)
            + jnp.einsum('bhqk,bkhe->bqhe', att[..., P:], v_new))

def conv_module(val, gate, buf, w, b, ln_g, ln_b):
    glu = val * jax.nn.sigmoid(gate)
    xp = jnp.concatenate([buf.astype(glu.dtype), glu], axis=1)
    y = lax.conv_general_dilated(xp, w[:, None, :].astype(xp.dtype), window_strides=(1,), padding='VALID',
                                 dimension_numbers=('NWC', 'WIO', 'NWC'), feature_group_count=B_WIDTH)
    y = layernorm(y + b.astype(y.dtype), ln_g, ln_b)
    return jax.nn.silu(y), xp[:, -(CONV_WIDTH - 1):]

def rwkv7_mix(u, shift_prev, S0, v_first, p, i):
    B, T, D = u.shape
    prev = jnp.concatenate([shift_prev[:, None, :].astype(u.dtype), u[:, :-1]], axis=1)
    xx = prev - u
    xm = u[:, :, None, :] + xx[:, :, None, :] * p['rwkv_mu'][i]
    xr, xw, xk, xv, xa, xg = [xm[:, :, j] for j in range(6)]
    r = xr @ p['rwkv_wr'][i]
    k = xk @ p['rwkv_wk'][i]
    v = xv @ p['rwkv_wv'][i]
    w = -jax.nn.softplus(-(p['rwkv_w0'][i] + jnp.tanh(xw @ p['rwkv_w1'][i]) @ p['rwkv_w2'][i])) - 0.5
    if v_first is None:
        v_first = v
    else:
        j = i - 1
        v = v + (v_first - v) * jax.nn.sigmoid(p['rwkv_v0'][j] + (xv @ p['rwkv_v1'][j]) @ p['rwkv_v2'][j])
    a = jax.nn.sigmoid(p['rwkv_a0'][i] + (xa @ p['rwkv_a1'][i]) @ p['rwkv_a2'][i])
    g = jax.nn.sigmoid(xg @ p['rwkv_g1'][i]) @ p['rwkv_g2'][i]

    def hs(t):
        return t.astype(F32).reshape(B, T, C_HEADS, C_HEAD)

    kk = hs(k * p['rwkv_kk'][i])
    kk = kk / jnp.maximum(jnp.sqrt(jnp.sum(kk * kk, axis=-1, keepdims=True)), 1e-12)
    k = k * (1 + (a - 1) * p['rwkv_ka'][i])
    rh, kh, vh, ah = hs(r), hs(k), hs(v), hs(a)
    decay = jnp.exp(-jnp.exp(hs(w)))

    def tm(t):
        return jnp.swapaxes(t, 0, 1)

    def step(S, inp):
        r_t, d_t, k_t, v_t, a_t, b_t = inp
        sa = jnp.einsum('bhij,bhj->bhi', S, a_t)
        S = S * d_t[:, :, None, :] + sa[..., None] * b_t[:, :, None, :] + v_t[..., None] * k_t[:, :, None, :]
        return S, jnp.einsum('bhij,bhj->bhi', S, r_t)

    S_T, ys = lax.scan(step, S0.astype(F32), (tm(rh), tm(decay), tm(kh), tm(vh), tm(-kk), tm(kk * ah)))
    ys = tm(ys)
    mean = jnp.mean(ys, axis=-1, keepdims=True)
    var = jnp.mean(jnp.square(ys - mean), axis=-1, keepdims=True)
    yn = ((ys - mean) * lax.rsqrt(var + GN_EPS)).reshape(B, T, D)
    yn = yn * p['rwkv_lnx_g'][i].astype(F32) + p['rwkv_lnx_b'][i].astype(F32)
    bonus = (jnp.sum(rh * kh * p['rwkv_rk'][i].astype(F32), axis=-1, keepdims=True) * vh).reshape(B, T, D)
    out = ((yn + bonus).astype(u.dtype) * g) @ p['rwkv_wo'][i]
    return out, u[:, -1], S_T.astype(S0.dtype), v_first

def trunk(x, pos, attend, conv_buf, wkv, shift, p):
    h = x
    Bn, T = x.shape[:2]
    new_k, new_v, new_conv, new_wkv, new_shift = [], [], [], [], []
    v_first = None
    splits = [A_WIDTH, 2 * A_WIDTH, 3 * A_WIDTH, 3 * A_WIDTH + B_WIDTH]
    for l in range(DEPTH):
        u = rmsnorm(h, p['norm_mix'][l])
        i = l // 2
        if l % 2 == 0:
            z = u @ p['w_in_ab'][i]
            q, k, v, gv, gg = jnp.split(z, splits, axis=-1)
            q = rope_partial(q.reshape(Bn, T, A_HEADS, 2, A_QK_DIM), pos)
            k = rope_partial(k.reshape(Bn, T, A_HEADS, 2, A_QK_DIM), pos)
            v = v.reshape(Bn, T, A_HEADS, A_V_DIM)
            lam, lam_init = diff_lambda(p['diff_lambda'][i], l)
            o = attend(i, q, k, v, lam)
            o = rmsnorm(o, p['subln'][i], SUBLN_EPS) * (1.0 - lam_init)
            c, buf = conv_module(gv, gg, conv_buf[i], p['conv_w'][i], p['conv_b'][i],
                                 p['conv_ln_g'][i], p['conv_ln_b'][i])
            mix = jnp.concatenate([o.reshape(Bn, T, A_WIDTH), c], axis=-1) @ p['w_out_ab'][i]
            new_k.append(k.reshape(Bn, T, A_HEADS, 2 * A_QK_DIM))
            new_v.append(v)
            new_conv.append(buf)
        else:
            mix, s_last, S_T, v_first = rwkv7_mix(u, shift[i], wkv[i], v_first, p, i)
            new_wkv.append(S_T)
            new_shift.append(s_last)
        h = h + mix
        f = rmsnorm(h, p['norm_ffn'][l])
        h = h + (jax.nn.silu(f @ p['w_gate'][l]) * (f @ p['w_up'][l])) @ p['w_down'][l]
    y = rmsnorm(h, p['norm_final'])
    return y, jnp.stack(new_k), jnp.stack(new_v), jnp.stack(new_conv), jnp.stack(new_wkv), jnp.stack(new_shift)

def setup_inputs(seed: int = 0) -> dict:
    key = jax.random.key(seed)
    ks = iter(jax.random.split(key, 64))

    def nrm(shape, scale):
        return jax.random.normal(next(ks), shape, F32) * scale

    D = D_MODEL
    n_pages = PAST_LEN // PAGE_SIZE
    n_used = DEC_BATCH * n_pages
    n_pool = n_used + max(1, n_used // 4)
    page_table = jax.random.permutation(next(ks), n_pool)[:n_used].reshape(DEC_BATCH, n_pages).astype(jnp.int32)
    return {
        'x_prompt': nrm((BATCH, SEQ, D), 1.0),
        'x_sample': nrm((DEC_BATCH, DEC_SEQ, D), 1.0),
        'cache_k': nrm((N_A_LAYERS, n_pool, PAGE_SIZE, A_HEADS, 2 * A_QK_DIM), 1.0),
        'cache_v': nrm((N_A_LAYERS, n_pool, PAGE_SIZE, A_HEADS, A_V_DIM), 1.0),
        'state_conv': nrm((N_A_LAYERS, DEC_BATCH, CONV_WIDTH - 1, B_WIDTH), 0.5),
        'state_wkv': nrm((N_C_LAYERS, DEC_BATCH, C_HEADS, C_HEAD, C_HEAD), 0.3),
        'state_shift': nrm((N_C_LAYERS, DEC_BATCH, D), 1.0),
        'page_table': page_table,
        'norm_mix': 1.0 + nrm((DEPTH, D), 0.05),
        'norm_ffn': 1.0 + nrm((DEPTH, D), 0.05),
        'norm_final': 1.0 + nrm((D,), 0.05),
        'w_in_ab': nrm((N_A_LAYERS, D, IN_AB), D ** -0.5),
        'diff_lambda': nrm((N_A_LAYERS, 4, A_QK_DIM), 0.1),
        'subln': 1.0 + nrm((N_A_LAYERS, A_V_DIM), 0.05),
        'conv_w': nrm((N_A_LAYERS, CONV_WIDTH, B_WIDTH), CONV_WIDTH ** -0.5),
        'conv_b': nrm((N_A_LAYERS, B_WIDTH), 0.02),
        'conv_ln_g': 1.0 + nrm((N_A_LAYERS, B_WIDTH), 0.05),
        'conv_ln_b': nrm((N_A_LAYERS, B_WIDTH), 0.02),
        'w_out_ab': nrm((N_A_LAYERS, D, D), D ** -0.5),
        'rwkv_mu': jax.random.uniform(next(ks), (N_C_LAYERS, 6, D), F32),
        'rwkv_wr': nrm((N_C_LAYERS, D, D), D ** -0.5),
        'rwkv_wk': nrm((N_C_LAYERS, D, D), D ** -0.5),
        'rwkv_wv': nrm((N_C_LAYERS, D, D), D ** -0.5),
        'rwkv_w0': -2.5 + nrm((N_C_LAYERS, D), 1.0),
        'rwkv_w1': nrm((N_C_LAYERS, D, LORA_DECAY), D ** -0.5),
        'rwkv_w2': nrm((N_C_LAYERS, LORA_DECAY, D), 0.1 * LORA_DECAY ** -0.5),
        'rwkv_a0': nrm((N_C_LAYERS, D), 0.1),
        'rwkv_a1': nrm((N_C_LAYERS, D, LORA_A), D ** -0.5),
        'rwkv_a2': nrm((N_C_LAYERS, LORA_A, D), 0.1 * LORA_A ** -0.5),
        'rwkv_v0': 1.0 + nrm((N_C_LAYERS - 1, D), 0.1),
        'rwkv_v1': nrm((N_C_LAYERS - 1, D, LORA_MV), D ** -0.5),
        'rwkv_v2': nrm((N_C_LAYERS - 1, LORA_MV, D), 0.1 * LORA_MV ** -0.5),
        'rwkv_g1': nrm((N_C_LAYERS, D, LORA_GATE), D ** -0.5),
        'rwkv_g2': nrm((N_C_LAYERS, LORA_GATE, D), LORA_GATE ** -0.5),
        'rwkv_kk': 0.85 + nrm((N_C_LAYERS, D), 0.05),
        'rwkv_ka': 1.0 + nrm((N_C_LAYERS, D), 0.05),
        'rwkv_rk': nrm((N_C_LAYERS, C_HEADS, C_HEAD), 0.1),
        'rwkv_lnx_g': 1.0 + nrm((N_C_LAYERS, D), 0.05),
        'rwkv_lnx_b': nrm((N_C_LAYERS, D), 0.02),
        'rwkv_wo': nrm((N_C_LAYERS, D, D), D ** -0.5),
        'w_gate': nrm((DEPTH, D, D_FF), D ** -0.5),
        'w_up': nrm((DEPTH, D, D_FF), D ** -0.5),
        'w_down': nrm((DEPTH, D_FF, D), D_FF ** -0.5),
    }

def reference(x_prompt, x_sample, cache_k, cache_v, state_conv, state_wkv, state_shift, page_table,
              norm_mix, norm_ffn, norm_final, w_in_ab, diff_lambda, subln, conv_w, conv_b, conv_ln_g, conv_ln_b,
              w_out_ab, rwkv_mu, rwkv_wr, rwkv_wk, rwkv_wv, rwkv_w0, rwkv_w1, rwkv_w2, rwkv_a0, rwkv_a1, rwkv_a2,
              rwkv_v0, rwkv_v1, rwkv_v2, rwkv_g1, rwkv_g2, rwkv_kk, rwkv_ka, rwkv_rk, rwkv_lnx_g, rwkv_lnx_b,
              rwkv_wo, w_gate, w_up, w_down):
    p = dict(norm_mix=norm_mix, norm_ffn=norm_ffn, norm_final=norm_final, w_in_ab=w_in_ab,
             diff_lambda=diff_lambda, subln=subln, conv_w=conv_w, conv_b=conv_b, conv_ln_g=conv_ln_g,
             conv_ln_b=conv_ln_b, w_out_ab=w_out_ab, rwkv_mu=rwkv_mu, rwkv_wr=rwkv_wr, rwkv_wk=rwkv_wk,
             rwkv_wv=rwkv_wv, rwkv_w0=rwkv_w0, rwkv_w1=rwkv_w1, rwkv_w2=rwkv_w2, rwkv_a0=rwkv_a0,
             rwkv_a1=rwkv_a1, rwkv_a2=rwkv_a2, rwkv_v0=rwkv_v0, rwkv_v1=rwkv_v1, rwkv_v2=rwkv_v2,
             rwkv_g1=rwkv_g1, rwkv_g2=rwkv_g2, rwkv_kk=rwkv_kk, rwkv_ka=rwkv_ka, rwkv_rk=rwkv_rk,
             rwkv_lnx_g=rwkv_lnx_g, rwkv_lnx_b=rwkv_lnx_b, rwkv_wo=rwkv_wo, w_gate=w_gate, w_up=w_up,
             w_down=w_down)

    Bp, Tp = x_prompt.shape[:2]
    dt = x_prompt.dtype
    zero_conv = jnp.zeros((N_A_LAYERS, Bp, CONV_WIDTH - 1, B_WIDTH), dt)
    zero_wkv = jnp.zeros((N_C_LAYERS, Bp, C_HEADS, C_HEAD, C_HEAD), dt)
    zero_shift = jnp.zeros((N_C_LAYERS, Bp, D_MODEL), dt)

    def attend_prompt(i, q, k, v, lam):
        return diff_attn_prompt(q, k, v, lam)

    y_prompt, nk_p, nv_p, nc_p, nw_p, ns_p = trunk(x_prompt, jnp.arange(Tp), attend_prompt,
                                                   zero_conv, zero_wkv, zero_shift, p)

    Bd, n_pages = page_table.shape
    past = n_pages * PAGE_SIZE

    def attend_sample(i, q, k, v, lam):
        kp = cache_k[i, page_table].reshape(Bd, past, A_HEADS, 2, A_QK_DIM)
        vp = cache_v[i, page_table].reshape(Bd, past, A_HEADS, A_V_DIM)
        return diff_attn_sample(q, k, v, kp, vp, lam)

    y_sample, nk_s, nv_s, nc_s, nw_s, ns_s = trunk(x_sample, past + jnp.arange(x_sample.shape[1]), attend_sample,
                                                   state_conv, state_wkv, state_shift, p)
    return (y_prompt, y_sample, nk_p, nv_p, nc_p, nw_p, ns_p, nk_s, nv_s, nc_s, nw_s, ns_s)


_drawn_inputs = setup_inputs


def setup_inputs(seed=0):
    import zlib

    import numpy as np

    out = dict(_drawn_inputs(seed))
    spreads = {}
    factors = {'conv_ln_b': 3.99,
     'rwkv_w1': 5.959,
     'rwkv_w2': 5.891,
     'rwkv_lnx_g': 2.731,
     'rwkv_lnx_b': 7.498}
    for name, (base, spread) in spreads.items():
        noise = np.random.default_rng([zlib.crc32(name.encode()), seed]).standard_normal(out[name].shape)
        drawn = base * np.exp(spread * noise) if base else spread * noise
        out[name] = __import__('jax').numpy.asarray(drawn.astype(out[name].dtype))
    for name, factor in factors.items():
        out[name] = (out[name] * factor).astype(out[name].dtype)
    return out
```

```python
import math
from contextlib import ExitStack

import numpy as np
import concourse.bass as bass
from concourse import mybir

F32 = mybir.dt.float32
ALU = mybir.AluOpType
ACT = mybir.ActivationFunctionType
AXX = mybir.AxisListType.X
ds = bass.ds

P = 128
D = 1024
KD = D // P
TP = 1024
NB, NT = 8, 4
TS = NB * NT
T = TP + TS
NCH = 3
TC = T // NCH
PAST, PAGE = 1024, 128
NPG = PAST // PAGE
NPOOL = NB * NPG + max(1, NB * NPG // 4)
AH = 4
DH = 64
CW = 31
LEAD = CW - 1
BT = 4
DFF = 2816
FT = DFF // P
PAIRS = 8
CL = 64
NC = TP // CL
LW, LG = 64, 160
NORM_EPS, SUBLN_EPS, LN_EPS, GN_EPS = 1e-6, 1e-5, 1e-5, 64e-5
NEG = -1.0e30
SCALE = DH ** -0.5
LAM_INIT = 0.8 - 0.6 * math.exp(-0.3 * 0)
START = 1
DECAY = math.exp(-0.5)


def chunk(n):
    return slice(n * TC, (n + 1) * TC)


class Columns:

    def __init__(self, blocks):
        self.at, self.n = {}, 0
        for name, width in blocks:
            self.at[name] = slice(self.n, self.n + width)
            self.n += width


CONST = Columns([
    ("ident", P), ("ones", P), ("headones", P), ("causal", P), ("rot", P),
    ("comb", 64), ("map", 2), ("newmask", 2 * TS), ("brow", NB),
    ("d_p", P), ("e_p", P), ("dT_p", P), ("a_p", P), ("q_p", CL),
    ("d_s", P), ("e_s", P), ("dT_s", P), ("a_s", P), ("q_s", CL),
])
VEC = Columns([
    ("mix", 2 * KD), ("ffn", 2 * KD), ("final", KD), ("conv_b", BT), ("cln_g", BT), ("cln_b", BT),
    ("subln", 1), ("mu", 6 * KD), ("w0", KD), ("a0", KD), ("kk", KD), ("ka", KD), ("rk", KD),
    ("lnx_g", KD), ("lnx_b", KD), ("conv_w", BT * CW), ("shift", KD * NB),
])


def constants():
    c = np.zeros((P, CONST.n), np.float32)
    i = np.arange(P)
    c[:, CONST.at["ident"]] = np.eye(P)
    c[:, CONST.at["ones"]] = 1
    c[:, CONST.at["headones"]] = i[:, None] // DH == i[None] // DH
    c[:, CONST.at["causal"]] = np.where(i[None] <= i[:, None], 0, NEG)
    rot = np.zeros((P, P), np.float32)
    for base in (0, DH):
        for d in range(8):
            rot[base + 8 + d, base + d] = -1
            rot[base + d, base + 8 + d] = 1
    c[:, CONST.at["rot"]] = rot
    b, h, t = i // 32, i // 8 % 4, i % 4
    row64 = b * 16 + h * 4 + t
    comb = np.zeros((P, 64), np.float32)
    comb[i, row64] = 1
    c[:, CONST.at["comb"]] = comb
    c[:, CONST.at["map"]] = (i // 4 % 2)[:, None] == np.arange(2)[None]
    k = np.arange(TS)
    for g in range(2):
        ok = (k[None] // NT == (4 * g + b)[:, None]) & (k[None] % NT <= t[:, None])
        c[:, CONST.at["newmask"].start + g * TS:][:, :TS] = np.where(ok, 0, NEG)
    hh, s = i // CL, i % CL
    c[:, CONST.at["brow"]] = (s[:, None] // NT == np.arange(NB)[None]) & (s[:, None] < TS)
    same = hh[:, None] == hh[None]
    S, U = s[:, None], s[None]
    for tag, size, blk in (("p", 16, CL), ("s", NT, NT)):
        inb = same & (S // size == U // size) & (S < U)
        out = same & (S // size != U // size) & (S < U) & (S // blk == U // blk)
        c[:, CONST.at["d_" + tag]] = inb
        c[:, CONST.at["e_" + tag]] = out
        c[:, CONST.at["dT_" + tag]] = inb.T
        c[:, CONST.at["a_" + tag]] = inb | out
        q = np.arange(CL)[None]
        c[:, CONST.at["q_" + tag]] = (S <= q) & (S // blk == q // blk)
    pos = np.concatenate([np.arange(TP), PAST + np.tile(np.arange(NT), NB)]).astype(np.float32)
    inv = (1.0 / (np.float32(500000.0) ** (np.arange(0, 16, 2, dtype=np.float32) / 16))).astype(np.float32)
    ang = pos[None] * inv[:, None]
    trig = np.zeros((P, 2 * T), np.float32)
    trig[:, :T] = 1
    for base in (0, 8, DH, DH + 8):
        trig[base:base + 8, :T] = np.cos(ang)
        trig[base:base + 8, T:] = np.sin(ang)
    keep = np.ones((P, T), np.float32)
    keep[:, 0:TP:CL] = 0
    keep[:, TP::NT] = 0
    return c, trig, keep


class Constants:

    def __init__(self, cst):
        def view(name):
            return cst[:, CONST.at[name]]

        self.ones, self.ident, self.rot = view("ones"), view("ident"), view("rot")
        self.causal, self.comb, self.headones = view("causal"), view("comb"), view("headones")
        self.map1, self.map2 = view("map")[:, 0:1], view("map")[:, 1:2]


class Stage:

    finished = []

    def __init__(self, nc, tag):
        self.nc, self.tag, self.stack, self.sems = nc, tag, ExitStack(), []

    def __enter__(self):
        if len(Stage.finished) > 60:
            self.nc.clear_and_free_semaphores(Stage.finished)
            self.nc.all_engine_barrier()
            Stage.finished = []
        self.stack.__enter__()
        return self

    def __exit__(self, *e):
        Stage.finished += self.sems
        return self.stack.__exit__(*e)

    def sb(self, name, shape, dt=F32):
        return self.stack.enter_context(self.nc.sbuf_tensor(f"{self.tag}_{name}", shape, dt))

    def bank(self, name, cols=512):
        return self.stack.enter_context(self.nc.psum_tensor(f"{self.tag}_{name}", [P, cols], F32))

    def sem(self, name):
        self.sems.append(self.nc.alloc_semaphore(f"{self.tag}_{name}"))
        return self.sems[-1]



def load_weight_tiles(sp, slots, source, loaded, chunk_done, tiles):
    for s in range(2):
        sp.dma_start(slots[:, s], source[s]).then_inc(loaded[s], 16)
    with sp.Fori(1, tiles // 2) as it:
        for s in range(2):
            sp.wait_ge(chunk_done, it * (2 * NCH) + (s - 1) * NCH)
            sp.dma_start(slots[:, s], source[ds(it * 2 + s, 1)][0]).then_inc(loaded[s], 16)


def multiply_tiles(pe, slots, rhs, kc, loaded, banks, bank_free, chunk_done, tiles):
    with pe.Fori(0, tiles // 2) as it:
        for s in range(2):
            pe.wait_ge(loaded[s], it * 16 + 16)
            for n in range(NCH):
                pe.wait_ge(bank_free[s], it * NCH + n + 1)
                for k in range(kc):
                    last = pe.matmul(banks[s * NCH + n][:, :TC], slots[:, s, k * P:(k + 1) * P],
                                     rhs(k, n), start=(k == 0), stop=(k == kc - 1))
                last.then_inc(chunk_done, 1)


class Dense(Stage):

    def __init__(self, nc, tag, kc):
        super().__init__(nc, tag)
        self.kc = kc

    def __enter__(self):
        super().__enter__()
        self.slots = self.sb("weights", [P, 2, self.kc * P])
        self.banks = [self.bank(f"out{i}") for i in range(2 * NCH)]
        self.loaded = [self.sem(f"weights_loaded{s}") for s in range(2)]
        self.chunk_done = self.sem("chunk_done")
        self.bank_free = [self.sem(f"bank_free{s}") for s in range(2)]
        return self

    def load(self, sp, source, tiles):
        load_weight_tiles(sp, self.slots, source, self.loaded, self.chunk_done, tiles)

    def multiply(self, pe, rhs, tiles):
        multiply_tiles(pe, self.slots, rhs, self.kc, self.loaded, self.banks, self.bank_free,
                       self.chunk_done, tiles)


def rms_norm(nc, tag, src, gain, dst, K):
    with Stage(nc, tag) as st:
        sq = st.sb("squares", [P, 2, T])
        rstd = st.sb("rstd", [P, T])
        inv = st.sb("inv", [P, T])
        sums = [st.bank(f"sum{n}") for n in range(NCH)]
        squared, summed, mean_ready = st.sem("squared"), st.sem("summed"), st.sem("mean_ready")
        inv_ready, rstd_ready = st.sem("inv_ready"), st.sem("rstd_ready")
        with nc.Block() as block:
            @block.scalar
            def _(act):
                for k in range(KD):
                    if k >= 2:
                        act.wait_ge(summed, k - 1)
                    act.activation(sq[:, k % 2], src[:, k], ACT.Square).then_inc(squared, 1)
                act.wait_ge(inv_ready, 1)
                act.activation(rstd[:], inv[:], ACT.Sqrt).then_inc(rstd_ready, 1)

            @block.tensor
            def _(pe):
                for k in range(KD):
                    pe.wait_ge(squared, k + 1)
                    for n in range(NCH):
                        last = pe.matmul(sums[n][:, :TC], K.ones, sq[:, k % 2, chunk(n)],
                                         start=(k == 0), stop=(k == KD - 1))
                    last.then_inc(summed, 1)

            @block.vector
            def _(dve):
                dve.wait_ge(summed, KD)
                for n in range(NCH):
                    dve.tensor_scalar(rstd[:, chunk(n)], sums[n][:, :TC], 1.0 / D, NORM_EPS,
                                      ALU.mult, ALU.add).then_inc(mean_ready, 1)
                dve.wait_ge(mean_ready, NCH)
                dve.reciprocal(inv[:], rstd[:]).then_inc(inv_ready, 1)
                dve.wait_ge(rstd_ready, 1)
                for k in range(KD):
                    dve.scalar_tensor_tensor(dst[:, k], src[:, k], gain[:, k:k + 1], rstd[:],
                                             ALU.mult, ALU.mult)


def add_projection(nc, tag, rhs, kc, source, hT):
    with Dense(nc, tag, kc) as st:
        added = st.sem("added")
        with nc.Block() as block:
            @block.sync
            def _(sp):
                st.load(sp, source, KD)

            @block.tensor
            def _(pe):
                st.multiply(pe, rhs, KD)

            @block.vector
            def _(dve):
                for s in range(2):
                    dve.sem_inc(st.bank_free[s], NCH)
                with dve.Fori(0, KD // 2) as it:
                    for s in range(2):
                        row = hT[:, ds(it * 2 + s, 1)]
                        for n in range(NCH):
                            dve.wait_ge(st.chunk_done, it * (2 * NCH) + s * NCH + n + 1)
                            out = row[:, 0, chunk(n)]
                            dve.tensor_tensor(out, st.banks[s * NCH + n][:, :TC], out,
                                              ALU.add).then_inc(st.bank_free[s], 1)


def gated_projection(nc, tag, rhs, source, tiles, func, dst, lead=0):
    with Dense(nc, tag, KD) as st:
        gate = st.sb("gate", [P, NCH, TC])
        gate_ready, product_done = st.sem("gate_ready"), st.sem("product_done")
        with nc.Block() as block:
            @block.sync
            def _(sp):
                st.load(sp, source, 2 * tiles)

            @block.tensor
            def _(pe):
                st.multiply(pe, rhs, 2 * tiles)

            @block.scalar
            def _(act):
                act.sem_inc(st.bank_free[0], NCH)
                with act.Fori(0, tiles) as it:
                    for n in range(NCH):
                        act.wait_ge(st.chunk_done, it * (2 * NCH) + n + 1)
                        act.wait_ge(product_done, it * NCH + n + 1)
                        act.activation(gate[:, n], st.banks[n][:, :TC], func).then_inc(st.bank_free[0], 1)
                        act.wait_ge(st.bank_free[0], it * NCH + n + 1 + NCH)
                        act.sem_inc(gate_ready, 1)

            @block.vector
            def _(dve):
                dve.sem_inc(product_done, NCH)
                dve.sem_inc(st.bank_free[1], NCH)
                with dve.Fori(0, tiles) as it:
                    row = dst[:, ds(it, 1)]
                    for n in range(NCH):
                        dve.wait_ge(st.chunk_done, it * (2 * NCH) + NCH + n + 1)
                        dve.wait_ge(gate_ready, it * NCH + n + 1)
                        dve.tensor_tensor(row[:, 0, lead + n * TC:lead + (n + 1) * TC],
                                          st.banks[NCH + n][:, :TC], gate[:, n],
                                          ALU.mult).then_inc(st.bank_free[1], 1)
                        dve.wait_ge(st.bank_free[1], it * NCH + n + 1 + NCH)
                        dve.sem_inc(product_done, 1)


def store_or_load(nc, tag, moves):
    with Stage(nc, tag) as st:
        moved = st.sem("moved")
        with nc.Block() as block:
            @block.sync
            def _(sp):
                for dst, src in moves:
                    sp.dma_start(dst, src).then_inc(moved, 16)
                sp.wait_ge(moved, 16 * len(moves))


def weight_tiles(w):
    k, m = w.shape
    return np.ascontiguousarray(w.reshape(k // P, P, m // P, P).transpose(2, 1, 0, 3).reshape(m // P, P, k))


def columns(v):
    return np.asarray(v, np.float32).reshape(-1, P).T


def channels(x):
    return np.ascontiguousarray(x.reshape(x.shape[0], -1, P).transpose(2, 1, 0))


def lay_out(i):
    i = {k: np.asarray(v) for k, v in i.items()}
    tok = np.concatenate([i["x_prompt"].reshape(TP, D), i["x_sample"].reshape(TS, D)])
    w_in = i["w_in_ab"][0]
    glu = np.stack([weight_tiles(w_in[:, 2048:]), weight_tiles(w_in[:, 1536:2048])], 1)
    vec = np.concatenate([
        columns(i["norm_mix"]), columns(i["norm_ffn"]), columns(i["norm_final"]), columns(i["conv_b"]),
        columns(i["conv_ln_g"]), columns(i["conv_ln_b"]), columns(i["subln"]), columns(i["rwkv_mu"]),
        columns(i["rwkv_w0"]), columns(i["rwkv_a0"]), columns(i["rwkv_kk"]), columns(i["rwkv_ka"]),
        columns(i["rwkv_rk"]), columns(i["rwkv_lnx_g"]), columns(i["rwkv_lnx_b"]),
        i["conv_w"][0].reshape(CW, BT, P).transpose(2, 1, 0).reshape(P, BT * CW),
        channels(i["state_shift"][0]).reshape(P, KD * NB)], 1)
    cst, trig, keep = constants()
    out = {
        "x": channels(tok), "cst": cst, "trig": trig, "keep": keep, "vec": np.ascontiguousarray(vec),
        "w_qk": weight_tiles(w_in[:, :1024]), "w_v": weight_tiles(w_in[:, 1024:1536]),
        "w_glu": glu.reshape(-1, P, D), "w_out": weight_tiles(i["w_out_ab"][0]),
        "lam": i["diff_lambda"].reshape(1, 4 * DH), "page_table": i["page_table"].reshape(1, -1),
        "cache_k": np.ascontiguousarray(i["cache_k"][0].transpose(0, 3, 2, 1)),
        "cache_v": i["cache_v"][0].reshape(NPOOL, PAGE, AH * P),
        "state_conv": np.ascontiguousarray(
            i["state_conv"][0].transpose(2, 0, 1).reshape(BT, P, NB, LEAD).transpose(1, 0, 2, 3)),
    }
    g1, g2 = i["rwkv_g1"][0], i["rwkv_g2"][0]
    flat = lambda w: np.ascontiguousarray(w.reshape(KD, P, -1).transpose(1, 0, 2).reshape(P, -1))
    wkv = i["state_wkv"][0].transpose(1, 3, 0, 2)
    out |= {
        "w_rkv": np.concatenate([weight_tiles(i[n][0]) for n in ("rwkv_wr", "rwkv_wk", "rwkv_wv")]),
        "w_wa1": np.concatenate([flat(i["rwkv_w1"][0]), flat(i["rwkv_a1"][0])], 1),
        "w_g1": flat(g1[:, :P])[None], "w_g1b": flat(g1[:, P:]),
        "w_wa2": np.ascontiguousarray(np.concatenate([i["rwkv_w2"][0], i["rwkv_a2"][0]]).reshape(P, KD, P).transpose(1, 0, 2)),
        "w_g2": np.ascontiguousarray(g2[:P].reshape(P, KD, P).transpose(1, 0, 2)),
        "w_g2b": np.ascontiguousarray(g2[P:].reshape(LG - P, KD, P).transpose(1, 0, 2)),
        "w_o": weight_tiles(i["rwkv_wo"][0]),
        "state_wkv": np.ascontiguousarray(wkv.reshape(PAIRS, P, NB, DH)),
    }
    for l in range(2):
        gu = np.stack([weight_tiles(i["w_gate"][l]), weight_tiles(i["w_up"][l])], 1)
        out[f"w_gu{l}"] = gu.reshape(-1, P, D)
        out[f"w_down{l}"] = weight_tiles(i["w_down"][l])
    return out


def scratch_buffers(nc):
    dram = {n: nc.dram_tensor("scratch_" + n, [KD, P, T], F32).ap() for n in ("a", "b", "k", "r", "bonus")}
    dram["rkv"] = nc.dram_tensor("scratch_rkv", [3 * KD, P, T], F32).ap()
    dram["v"] = dram["rkv"][2 * KD:]
    return dram


TAPS_DVE = 17


def rotary_projection(nc, tag, uT, source, trig, K, dst, glu, vec):
    with Dense(nc, tag, KD) as st:
        cos, sin = trig[:, :T], trig[:, T:]
        raw = st.sb("raw", [P, NCH, TC])
        plain = st.sb("plain", [P, NCH, TC])
        turned = st.sb("turned", [P, NCH, TC])
        partner = [st.bank(f"partner{i}") for i in range(2)]
        raw_ready, cos_done, partner_ready = st.sem("raw_ready"), st.sem("cos_done"), st.sem("partner_ready")
        turn_done, stored = st.sem("turn_done"), st.sem("dst_written")
        acc, acc_b = st.sb("conv_acc", [P, TP]), st.sb("conv_acc_b", [P, TP])
        term = st.sb("conv_term", [P, 2, TP])
        tap, term_ready, term_added, conv_done = (st.sem(n) for n in ("tap", "term_ready", "term_added", "conv_done"))
        w_conv = vec[:, VEC.at["conv_w"]]
        TB_ = CW - TAPS_DVE

        def window(it, k):
            return glu[:, ds(it, 1), k:k + TP][:, 0]

        def weight(it, k):
            return w_conv[:, ds(it * CW + k, 1)]
        with nc.Block() as block:
            @block.sync
            def _(sp):
                st.load(sp, source, 2 * AH)

            @block.tensor
            def _(pe):
                with pe.Fori(0, AH) as it:
                    for s in range(2):
                        pe.wait_ge(st.loaded[s], it * 16 + 16)
                        for n in range(NCH):
                            pe.wait_ge(st.bank_free[s], it * NCH + n + 1)
                            for k in range(KD):
                                last = pe.matmul(st.banks[s * NCH + n][:, :TC],
                                                 st.slots[:, s, k * P:(k + 1) * P],
                                                 uT[:, k, chunk(n)], start=(k == 0), stop=(k == KD - 1))
                            last.then_inc(st.chunk_done, 1)
                        for n in range(NCH):
                            j = it * (2 * NCH) + s * NCH + n
                            pe.wait_ge(raw_ready, j + 1)
                            pe.wait_ge(turn_done, j + 1)
                            pe.matmul(partner[(s * NCH + n) % 2][:, :TC], K.rot, raw[:, n],
                                      start=True, stop=True).then_inc(partner_ready, 1)

            @block.scalar
            def _(act):
                for s in range(2):
                    act.sem_inc(st.bank_free[s], NCH)
                with act.Fori(0, AH) as it:
                    for s in range(2):
                        for n in range(NCH):
                            for e in range(TB_ * (s * NCH + n) // 6, TB_ * (s * NCH + n + 1) // 6):
                                act.wait_ge(term_added, it * TB_ + e + 1)
                                act.activation(term[:, e % 2], window(it, TAPS_DVE + e), ACT.Copy,
                                               scale=weight(it, TAPS_DVE + e)).then_inc(term_ready, 1)
                            j = it * (2 * NCH) + s * NCH + n
                            act.wait_ge(st.chunk_done, j + 1)
                            act.wait_ge(stored, j + 1)
                            act.activation(raw[:, n], st.banks[s * NCH + n][:, :TC],
                                           ACT.Copy).then_inc(st.bank_free[s], 1)
                            act.wait_ge(st.bank_free[s], it * NCH + n + 1 + NCH)
                            act.sem_inc(raw_ready, 1)

            @block.gpsimd
            def _(pool):
                pool.sem_inc(term_added, 2)
                with pool.Fori(0, AH) as it:
                    pool.wait_ge(term_ready, it * TB_ + 2)
                    pool.wait_ge(conv_done, START + it)
                    pool.tensor_tensor(acc_b[:], term[:, 0], term[:, 1], ALU.add).then_inc(term_added, 2)
                    for e in range(2, TB_):
                        pool.wait_ge(term_ready, it * TB_ + e + 1)
                        pool.wait_ge(term_added, it * TB_ + e + 2)
                        pool.tensor_tensor(acc_b[:], acc_b[:], term[:, e % 2], ALU.add).then_inc(term_added, 1)

            @block.vector
            def _(dve):
                dve.sem_inc(turn_done, 2)
                dve.sem_inc(stored, NCH)
                dve.sem_inc(conv_done, START)
                with dve.Fori(0, AH) as it:
                    for s in range(2):
                        row = dst[:, ds(it * 2 + s, 1)]
                        for n in range(NCH):
                            for k in range(TAPS_DVE * (s * NCH + n) // 6, TAPS_DVE * (s * NCH + n + 1) // 6):
                                if k == 0:
                                    dve.wait_ge(conv_done, START + it)
                                    dve.tensor_scalar(acc[:], window(it, 0), weight(it, 0), None,
                                                      ALU.mult).then_inc(tap, 1)
                                else:
                                    dve.wait_ge(tap, it * TAPS_DVE + k)
                                    dve.scalar_tensor_tensor(acc[:], window(it, k), weight(it, k), acc[:],
                                                             ALU.mult, ALU.add).then_inc(tap, 1)
                            j = it * (2 * NCH) + s * NCH + n
                            dve.wait_ge(raw_ready, j + 1)
                            dve.tensor_tensor(plain[:, n], raw[:, n], cos[:, chunk(n)], ALU.mult).then_inc(cos_done, 1)
                            dve.wait_ge(partner_ready, j + 1)
                            dve.tensor_tensor(turned[:, n], partner[(s * NCH + n) % 2][:, :TC],
                                              sin[:, chunk(n)], ALU.mult).then_inc(turn_done, 1)
                            dve.wait_ge(cos_done, j + 1)
                            dve.wait_ge(turn_done, j + 1 + 2)
                            dve.tensor_tensor(row[:, 0, chunk(n)], plain[:, n], turned[:, n],
                                              ALU.add).then_inc(stored, 1)
                    dve.wait_ge(tap, it * TAPS_DVE + TAPS_DVE)
                    dve.wait_ge(term_added, it * TB_ + TB_ + 2)
                    dve.tensor_tensor(window(it, 0), acc[:], acc_b[:], ALU.add).then_inc(conv_done, 1)


def plain_projection(nc, tag, rhs, source, tiles, dst):
    with Dense(nc, tag, KD) as st:
        with nc.Block() as block:
            @block.sync
            def _(sp):
                st.load(sp, source, tiles)

            @block.tensor
            def _(pe):
                st.multiply(pe, rhs, tiles)

            @block.scalar
            def _(act):
                for s in range(2):
                    act.sem_inc(st.bank_free[s], NCH)
                with act.Fori(0, tiles // 2) as it:
                    for s in range(2):
                        row = dst[:, ds(it * 2 + s, 1)]
                        for n in range(NCH):
                            act.wait_ge(st.chunk_done, it * (2 * NCH) + s * NCH + n + 1)
                            act.activation(row[:, 0, chunk(n)], st.banks[s * NCH + n][:, :TC],
                                           ACT.Copy).then_inc(st.bank_free[s], 1)


def keys_values_out(nc, qkT, vT, V, glu, glu_s, conv_s, lam, vec, K, A, O):
    with Stage(nc, "kvo") as st:
        tp = [st.bank(f"turn{i}") for i in range(4)]
        lb = st.bank("lam_bank")
        lamrow = st.sb("lamrow", [1, 4 * DH])
        prod = st.sb("lamprod", [1, 2, DH])
        terms = st.sb("conv_terms", [P, NB, NT, CW])
        termed, summed = st.sem("conv_terms_ready"), st.sem("conv_summed")
        dots = st.sb("lamdots", [1, 4])
        turned, copied = st.sem("turned"), st.sem("copied")
        stored, lam_in, buf_in = st.sem("stored"), st.sem("lambda_loaded"), st.sem("conv_state_loaded")
        zeroed, news = st.sem("lead_zeroed"), st.sem("new_rows_copied")
        l1, l2, l3, l4, l5, l6 = (st.sem(f"lambda_step{i}") for i in range(6))
        with nc.Block() as block:
            @block.sync
            def _(sp):
                sp.dma_start(lamrow[:], A["lam"]).then_inc(lam_in, 16)
                for c in range(BT):
                    sp.dma_start(glu_s[:, c, :, :LEAD], A["state_conv"][:, c]).then_inc(buf_in, 16)
                sp.dma_start(O["k"], qkT[:, AH:]).then_inc(stored, 16)
                sp.dma_start(O["v"], vT[:]).then_inc(stored, 16)
                sp.wait_ge(buf_in, 16 * BT)
                sp.wait_ge(news, BT)
                for c in range(BT):
                    sp.dma_start(O["conv_s"][:, c], glu_s[:, c, :, NT:]).then_inc(stored, 16)
                sp.wait_ge(stored, 16 * (2 + BT))

            @block.gpsimd
            def _(pool):
                for c in range(BT):
                    pool.tensor_copy(glu_s[:, c, :, LEAD:],
                                     glu[:, c, LEAD + TP:].rearrange("p (b t) -> p b t", t=NT)).then_inc(news, 1)

            @block.tensor
            def _(pe):
                for i in range(TP // P + 1):
                    if i >= 4:
                        pe.wait_ge(copied, i - 3)
                    n = P if i < TP // P else TS
                    for h in range(AH):
                        last = pe.transpose(tp[i % 4][:n, h * P:(h + 1) * P], vT[:, h, i * P:i * P + n], K.ident)
                    last.then_inc(turned, 1)
                pe.wait_ge(l4, 1)
                pe.matmul(lb[:, 0:2], K.ones[0:1], dots[0:1, 2:4], start=True, stop=True).then_inc(l5, 1)

            @block.vector
            def _(dve):
                for i in range(TP // P + 1):
                    n = P if i < TP // P else TS
                    dve.wait_ge(turned, i + 1)
                    dve.tensor_copy(V[:n, i], tp[i % 4][:n, :]).then_inc(copied, 1)
                dve.wait_ge(lam_in, 16)
                pair = lamrow[:].rearrange("p (a b d) -> p a b d", a=2, b=2)
                dve.tensor_tensor(prod[:], pair[:, :, 0], pair[:, :, 1], ALU.mult).then_inc(l1, 1)
                dve.wait_ge(l1, 1)
                dve.tensor_reduce(dots[:, 0:2], prod[:], AXX, ALU.add).then_inc(l2, 1)
                dve.wait_ge(l5, 1)
                dve.tensor_copy(lam[:, 1:3], lb[:, 0:2]).then_inc(l6, 1)
                dve.wait_ge(l6, 1)
                dve.scalar_tensor_tensor(lam[:, 0:1], lam[:, 2:3], -LAM_INIT, lam[:, 1:2], ALU.add, ALU.subtract)

                w = vec[:, VEC.at["conv_w"]].rearrange("p (c k) -> p c k", k=CW)
                dve.wait_ge(buf_in, 16 * BT)
                dve.wait_ge(news, BT)
                for c in range(BT):
                    if c:
                        dve.wait_ge(summed, c)
                    for t in range(NT):
                        dve.tensor_tensor(terms[:, :, t], glu_s[:, c, :, t:t + CW],
                                          w[:, c].unsqueeze(1).broadcast_to([P, NB, CW]), ALU.mult).then_inc(termed, 1)
                    dve.wait_ge(termed, (c + 1) * NT)
                    dve.tensor_reduce(conv_s[:, c], terms[:].rearrange("p b t k -> p (b t) k"), AXX,
                                      ALU.add).then_inc(summed, 1)

            @block.scalar
            def _(act):
                act.wait_ge(l2, 1)
                act.activation(dots[:, 2:4], dots[:, 0:2], ACT.Exp).then_inc(l4, 1)


def prompt_attention(nc, qkT, V, lam, mixT, K):
    NQ = TP // P
    with Stage(nc, "att") as st:
        qh, kh = st.sb("q_head", [P, TP]), st.sb("k_head", [P, TP])
        vh = st.sb("v_head", [P, NQ, P])
        pr = [[st.sb(f"prob{m}{b}", [P, TP]) for b in range(2)] for m in range(2)]
        att = [st.sb(f"att{b}", [P, TP]) for b in range(2)]
        attT = [st.sb(f"attT{b}", [P, NQ, P]) for b in range(2)]
        nmax, l, rl = st.sb("nmax", [P, 4]), st.sb("l", [P, 4]), st.sb("rl", [P, 4])
        coef = st.sb("coef", [P, 2])
        S = [st.bank(f"scores{m}", 1024) for m in range(2)]
        TB = st.bank("att_turned", 1024)
        OB = [st.bank(f"out{b}") for b in range(2)]
        staged, head_done = st.sem("head_staged"), st.sem("head_done")
        scored = [st.sem(f"scored{m}") for m in range(2)]
        maxed = [st.sem(f"maxed{m}") for m in range(2)]
        exped = [st.sem(f"exped{m}") for m in range(2)]
        recip, coefd, scaled, mixed = st.sem("recip"), st.sem("coef_ready"), st.sem("scaled"), st.sem("att_mixed")
        turned, turn_copied, summed, out_copied = st.sem("turned"), st.sem("turn_copied"), st.sem("summed"), st.sem("out_copied")
        with nc.Block() as block:
            @block.tensor
            def _(pe):
                def scores(h, i):
                    u = h * NQ + i
                    nk = (i + 1) * P
                    for m in range(2):
                        pe.wait_ge(exped[m], START + u)
                        rows = slice(m * DH, (m + 1) * DH)
                        for c in range(0, nk, 512):
                            w = min(512, nk - c)
                            pe.matmul(S[m][:, c:c + w], qh[rows, i * P:(i + 1) * P], kh[rows, c:c + w],
                                      start=True, stop=(c + w < nk))
                        pe.matmul(S[m][:, i * P:nk], K.ident, K.causal, start=False, stop=True).then_inc(scored[m], 1)

                def weigh(h, i):
                    u = h * NQ + i
                    pe.wait_ge(mixed, START + u + 1)
                    pe.wait_ge(turn_copied, START + u)
                    for b in range(i + 1):
                        last = pe.transpose(TB[:, b * P:(b + 1) * P], att[i % 2][:, b * P:(b + 1) * P], K.ident)
                    last.then_inc(turned, 1)
                    pe.wait_ge(turn_copied, START + u + 1)
                    if i >= 2:
                        pe.wait_ge(out_copied, START + u - 1)
                    for b in range(i + 1):
                        last = pe.matmul(OB[i % 2][:, :P], vh[:, b], attT[i % 2][:, b],
                                         start=(b == 0), stop=(b == i))
                    last.then_inc(summed, 1)

                pe.sem_inc(summed, START)
                with pe.Fori(0, AH) as h:
                    pe.wait_ge(staged, h * 3 + 3)
                    pe.wait_ge(out_copied, START + h * NQ)
                    scores(h, 0)
                    scores(h, 1)
                    for i in range(NQ):
                        if i + 2 < NQ:
                            scores(h, i + 2)
                        weigh(h, i)

            @block.vector
            def _(dve):
                def softmax_max(h, i):
                    u = h * NQ + i
                    for m in range(2):
                        dve.wait_ge(scored[m], u + 1)
                        if i >= 2:
                            dve.wait_ge(exped[m], START + u - 1)
                        c = 2 * m + i % 2
                        dve.tensor_reduce(nmax[:, c:c + 1], S[m][:, :(i + 1) * P], AXX, ALU.max,
                                          negate=True).then_inc(maxed[m], 1)

                def mix(h, i):
                    u = h * NQ + i
                    b, nk = i % 2, (i + 1) * P
                    for m in range(2):
                        dve.wait_ge(exped[m], START + u + 1)
                        c = 2 * m + b
                        dve.reciprocal(rl[:, c:c + 1], l[:, c:c + 1]).then_inc(recip, 1)
                    dve.wait_ge(recip, u * 2 + 2)
                    dve.tensor_scalar(coef[:, b:b + 1], rl[:, 2 + b:3 + b], lam[:, 0:1], None, ALU.mult).then_inc(coefd, 1)
                    if i >= 2:
                        dve.wait_ge(turned, u - 1)
                    dve.tensor_scalar(att[b][:, :nk], pr[0][b][:, :nk], rl[:, b:b + 1], None, ALU.mult).then_inc(scaled, 1)
                    dve.wait_ge(coefd, u + 1)
                    dve.wait_ge(scaled, u + 1)
                    dve.scalar_tensor_tensor(att[b][:, :nk], pr[1][b][:, :nk], coef[:, b:b + 1], att[b][:, :nk],
                                             ALU.mult, ALU.add).then_inc(mixed, 1)

                def out(h, i):
                    u = h * NQ + i
                    dve.wait_ge(summed, START + u + 1)
                    dve.tensor_copy(mixT[:, ds(h, 1), i * P:(i + 1) * P][:, 0], OB[i % 2][:, :P]).then_inc(out_copied, 1)

                dve.sem_inc(mixed, START)
                dve.sem_inc(out_copied, START)
                with dve.Fori(0, AH) as h:
                    dve.wait_ge(summed, START + h * NQ)
                    dve.tensor_scalar(qh[:], qkT[:, ds(h, 1), 0:TP][:, 0], SCALE, None, ALU.mult).then_inc(staged, 1)
                    dve.tensor_copy(kh[:], qkT[:, ds(h + AH, 1), 0:TP][:, 0]).then_inc(staged, 1)
                    dve.tensor_copy(vh[:], V[:, 0:NQ, ds(h * P, P)]).then_inc(staged, 1)
                    softmax_max(h, 0)
                    for i in range(NQ):
                        if i + 1 < NQ:
                            softmax_max(h, i + 1)
                        mix(h, i)
                        if i >= 2:
                            out(h, i - 2)
                    out(h, NQ - 2)
                    out(h, NQ - 1)

            @block.scalar
            def _(act):
                def exps(h, i):
                    u = h * NQ + i
                    nk, b = (i + 1) * P, i % 2
                    for m in range(2):
                        c = 2 * m + b
                        act.wait_ge(maxed[m], u + 1)
                        if i >= 2:
                            act.wait_ge(mixed, START + u - 1)
                        act.activation(pr[m][b][:, :nk], S[m][:, :nk], ACT.Exp, bias=nmax[:, c:c + 1],
                                       accum_out=l[:, c:c + 1]).then_inc(exped[m], 1)

                def copy_turned(h, i):
                    u = h * NQ + i
                    act.wait_ge(turned, u + 1)
                    act.activation(attT[i % 2][:, 0:i + 1], TB[:, :(i + 1) * P], ACT.Copy).then_inc(turn_copied, 1)

                for m in range(2):
                    act.sem_inc(exped[m], START)
                act.sem_inc(turn_copied, START)
                with act.Fori(0, AH) as h:
                    act.wait_ge(mixed, START + h * NQ)
                    act.wait_ge(summed, START + h * NQ)
                    exps(h, 0)
                    exps(h, 1)
                    for i in range(NQ):
                        if i + 2 < NQ:
                            exps(h, i + 2)
                        copy_turned(h, i)


def sample_attention(nc, qkT, V, lam, mixT, K, cst, A):
    HB = NB // 2
    with Stage(nc, "sat") as st:
        table = st.sb("page_table", [1, NB * NPG], mybir.dt.int32)
        kp, vp = (st.sb(n, [P, 4, AH * P * 2]) for n in ("k_pages", "v_pages"))
        vnew = st.sb("v_new", [TS, AH * P])
        qpad = st.sb("q_padded", [P, HB, AH, P])
        prob = st.sb("prob", [P, PAST + TS])
        nmax, l, rl = st.sb("nmax", [P, 1]), st.sb("l", [P, 1]), st.sb("rl", [P, 1])
        sign = st.sb("row_coef", [P, 1])
        attT = st.sb("attT", [P, NPG + 1, 64])
        S = st.bank("scores", 1024)
        SN = st.bank("scores_new")
        TB = st.bank("att_turned", 1024)
        OB = [st.bank(f"out{g}") for g in range(2)]
        table_in, zeroed, q_set = st.sem("table_loaded"), st.sem("q_zeroed"), st.sem("q_set")
        k_in, v_in = ([st.sem(f"{n}_in_slot{i}") for i in range(4)] for n in "kv")
        k_read, v_read = st.sem("k_slot_read"), st.sem("v_slot_read")
        scored, masked, maxed, exped, recip, coefd, scaled = (st.sem(n) for n in
            ("scored", "masked", "maxed", "exped", "recip", "coef_ready", "scaled"))
        turned, turn_copied, summed, out_copied = (st.sem(n) for n in
            ("turned", "turn_copied", "summed", "out_copied"))
        sign_ready = st.sem("row_coef_ready")
        HP = NPG // 2
        with nc.Block() as block:
            def load_pages(eng, name, in_slot, slot_read, place):
                with eng.Fori(0, NB) as b:
                    for hp in range(HP):
                        eng.wait_ge(slot_read, b * HP + hp + 1)
                        for j in range(2):
                            at = eng.value_load(table[0:1, ds(b * NPG + 2 * hp + j, 1)], min_val=0, max_val=NPOOL - 1)
                            eng.dma_start(place(hp, j), A[name][ds(at, 1)][0]).then_inc(in_slot[hp], 16)

            @block.sync
            def _(sp):
                sp.dma_start(table[:], A["page_table"]).then_inc(table_in, 16)
                sp.wait_ge(table_in, 16)
                load_pages(sp, "cache_k", k_in, k_read,
                           lambda hp, j: kp[:, hp].rearrange("p (h j k) -> p h j k", h=AH, j=2)[:, :, j])

            @block.gpsimd
            def _(pool):
                pool.memset(qpad[:], 0.0).then_inc(zeroed, 1)
                pool.wait_ge(table_in, 16)
                load_pages(pool, "cache_v", v_in, v_read,
                           lambda hp, j: vp[:, hp].rearrange("p (j c) -> p j c", j=2)[:, j])

            @block.tensor
            def _(pe):
                pe.sem_inc(k_read, 4)
                pe.sem_inc(v_read, 4)
                for g in range(2):
                    pe.wait_ge(q_set, g + 1)
                    if g:
                        pe.wait_ge(exped, g)
                    for b in range(HB):
                        for hp in range(HP):
                            pe.wait_ge(k_in[hp], 32 * (g * HB + b + 1))
                            for h in range(AH):
                                last = pe.matmul(S[:, hp * 256:(hp + 1) * 256], qpad[:, b, h],
                                                 kp[:, hp, h * 256:(h + 1) * 256],
                                                 start=(b == 0 and h == 0 and hp % 2 == 0),
                                                 stop=(b == HB - 1 and h == AH - 1), skip_group_check=True)
                            last.then_inc(k_read, 1)
                    for b in range(HB):
                        for h in range(AH):
                            last = pe.matmul(SN[:, :TS], qpad[:, b, h], qkT[:, AH + h, TP:T],
                                             start=(b == 0 and h == 0), stop=(b == HB - 1 and h == AH - 1))
                    last.then_inc(scored, 1)
                    pe.wait_ge(scaled, g + 1)
                    for j in range(NPG + 1):
                        n = P if j < NPG else TS
                        last = pe.matmul(TB[:n, j * 64:(j + 1) * 64], prob[:, j * P:j * P + n], K.comb,
                                         start=True, stop=True)
                    last.then_inc(turned, 1)
                    pe.wait_ge(turn_copied, g + 1)
                    for b in range(HB):
                        for hp in range(HP):
                            pe.wait_ge(v_in[hp], 32 * (g * HB + b + 1))
                            for j in range(2):
                                for h in range(AH):
                                    col, c0 = b * 16 + h * NT, j * AH * P + h * P
                                    last = pe.matmul(OB[g][:, col:col + NT], vp[:, hp, c0:c0 + P],
                                                     attT[:, 2 * hp + j, col:col + NT],
                                                     start=(b == 0 and hp == 0 and j == 0 and h == 0), stop=False,
                                                     skip_group_check=True)
                            last.then_inc(v_read, 1)
                        for h in range(AH):
                            col = b * 16 + h * NT
                            last = pe.matmul(OB[g][:, col:col + NT], V[:TS, NPG, h * P:(h + 1) * P],
                                             attT[:TS, NPG, col:col + NT], start=False,
                                             stop=True, skip_group_check=True)
                    last.then_inc(summed, 1)

            @block.vector
            def _(dve):
                for g in range(2):
                    dve.wait_ge(zeroed, 1)
                    if g:
                        dve.wait_ge(scored, g)
                    n = 0
                    for b in range(HB):
                        for m in range(2):
                            rows = slice(m * DH, (m + 1) * DH)
                            for h in range(AH):
                                col = b * 32 + h * 8 + m * NT
                                tok = TP + (g * HB + b) * NT
                                last = dve.tensor_scalar(qpad[rows, b, h, col:col + NT], qkT[rows, h, tok:tok + NT],
                                                         SCALE, None, ALU.mult)
                    last.then_inc(q_set, 1)
                    dve.wait_ge(scored, g + 1)
                    dve.tensor_tensor(prob[:, PAST:], SN[:, :TS], cst[:, CONST.at["newmask"]][:, g * TS:(g + 1) * TS],
                                      ALU.add).then_inc(masked, 1)
                    dve.tensor_reduce(nmax[:], S[:], AXX, ALU.max, negate=True).then_inc(masked, 1)
                    dve.wait_ge(masked, 4 * g + 2)
                    dve.tensor_reduce(rl[:], prob[:, PAST:], AXX, ALU.max, negate=True).then_inc(masked, 1)
                    dve.wait_ge(masked, 4 * g + 3)
                    dve.tensor_tensor(nmax[:], nmax[:], rl[:], ALU.min).then_inc(masked, 1)
                    dve.wait_ge(masked, 4 * g + 4)
                    dve.sem_inc(maxed, 1)
                    dve.wait_ge(exped, g + 1)
                    dve.tensor_tensor(l[:], l[:], sign[:], ALU.add).then_inc(coefd, 1)
                    dve.wait_ge(coefd, 4 * g + 1)
                    dve.reciprocal(rl[:], l[:]).then_inc(coefd, 1)
                    dve.wait_ge(coefd, 4 * g + 2)
                    dve.tensor_scalar(l[:], K.map2, lam[:, 0:1], None, ALU.mult).then_inc(coefd, 1)
                    dve.wait_ge(coefd, 4 * g + 3)
                    dve.scalar_tensor_tensor(l[:], l[:], K.map1, rl[:], ALU.add, ALU.mult).then_inc(coefd, 1)
                    dve.wait_ge(coefd, 4 * g + 4)
                    dve.tensor_scalar(prob[:], prob[:], l[:], None, ALU.mult).then_inc(scaled, 1)
                    dve.wait_ge(turned, g + 1)
                    dve.tensor_copy(attT[:, 0:NPG], TB[:, :NPG * 64])
                    dve.tensor_copy(attT[:TS, NPG], TB[:TS, NPG * 64:(NPG + 1) * 64]).then_inc(turn_copied, 1)
                    dve.wait_ge(summed, g + 1)
                    for h in range(AH):
                        tok = TP + g * HB * NT
                        last = dve.tensor_copy(
                            mixT[:, h, tok:tok + HB * NT].rearrange("p (b t) -> p b t", t=NT),
                            OB[g][:, :64].rearrange("p (b h t) -> p b h t", h=AH, t=NT)[:, :, h])
                    last.then_inc(out_copied, 1)

            @block.scalar
            def _(act):
                for g in range(2):
                    act.wait_ge(maxed, g + 1)
                    act.activation(prob[:, PAST:], prob[:, PAST:], ACT.Exp, bias=nmax[:],
                                   accum_out=l[:]).then_inc(recip, 1)
                    act.activation(prob[:, :PAST], S[:], ACT.Exp, bias=nmax[:], accum_out=sign[:]).then_inc(recip, 1)
                    act.wait_ge(recip, 2 * g + 2)
                    act.sem_inc(exped, 1)


def finish_mix(nc, mixT, glu, K, vec):
    with Stage(nc, "fin") as st:
        sq = st.sb("squares", [P, 2, T])
        stat = st.sb("stat", [P, 2, T])
        mean = st.sb("mean", [P, T])
        gain = st.sb("subln_gain", [P, 1])
        banks = [[st.bank(f"sum{s}{n}") for n in range(NCH)] for s in range(2)]
        squared, summed, taken, inv, rooted, read = (st.sem(n) for n in
            ("squared", "summed", "taken", "inverted", "rooted", "stat_read"))
        meaned, centred, shifted, gain_ready = st.sem("meaned"), st.sem("centred"), st.sem("shifted"), st.sem("gain_ready")
        sub = vec[:, VEC.at["subln"]]
        cb, cg, cbt = (vec[:, VEC.at[n]] for n in ("conv_b", "cln_g", "cln_b"))
        with nc.Block() as block:
            @block.tensor
            def _(pe):
                for h in range(AH):
                    pe.wait_ge(squared, h + 1)
                    if h >= 2:
                        pe.wait_ge(taken, h - 1)
                    for n in range(NCH):
                        last = pe.matmul(banks[h % 2][n][:, :TC], K.ones, sq[:, h % 2, chunk(n)], start=True, stop=True)
                    last.then_inc(summed, 1)
                pe.wait_ge(shifted, 2 * BT)
                pe.wait_ge(taken, AH - 1)
                for n in range(NCH):
                    for c in range(BT):
                        last = pe.matmul(banks[0][n][:, :TC], K.ones, mixT[:, AH + c, chunk(n)],
                                         start=(c == 0), stop=(c == BT - 1))
                last.then_inc(summed, 1)
                pe.wait_ge(taken, AH)
                for c in range(BT):
                    pe.wait_ge(squared, AH + c + 1)
                    for n in range(NCH):
                        last = pe.matmul(banks[1][n][:, :TC], K.ones, sq[:, c % 2, chunk(n)],
                                         start=(c == 0), stop=(c == BT - 1))
                    last.then_inc(summed, 1)

            @block.scalar
            def _(act):
                for h in range(AH):
                    if h >= 2:
                        act.wait_ge(summed, h - 1)
                    act.activation(sq[:, h % 2], mixT[:, h], ACT.Square).then_inc(squared, 1)
                for h in range(AH):
                    act.wait_ge(inv, h + 1)
                    act.activation(stat[:, h % 2], stat[:, h % 2], ACT.Sqrt).then_inc(rooted, 1)
                for c in range(BT):
                    act.wait_ge(centred, c + 1)
                    act.wait_ge(summed, AH + 1 + (c - 1 if c >= 2 else 0))
                    act.activation(sq[:, c % 2], mixT[:, AH + c], ACT.Square).then_inc(squared, 1)
                act.wait_ge(inv, AH + 1)
                act.activation(stat[:, 0], stat[:, 0], ACT.Sqrt).then_inc(rooted, 1)
                for c in range(BT):
                    act.wait_ge(read, AH + c + 1)
                    act.activation(mixT[:, AH + c], mixT[:, AH + c], ACT.Silu,
                                   bias=cbt[:, c:c + 1], scale=cg[:, c:c + 1])

            @block.vector
            def _(dve):
                dve.tensor_scalar(gain[:], sub, 1.0 - LAM_INIT, None, ALU.mult).then_inc(gain_ready, 1)
                for c in range(BT):
                    dve.tensor_scalar(mixT[:, AH + c, :TP], glu[:, c, :TP], cb[:, c:c + 1], None, ALU.add).then_inc(shifted, 1)
                    dve.tensor_scalar(mixT[:, AH + c, TP:], mixT[:, AH + c, TP:], cb[:, c:c + 1], None,
                                      ALU.add).then_inc(shifted, 1)
                for h in range(AH):
                    dve.wait_ge(summed, h + 1)
                    if h >= 2:
                        dve.wait_ge(read, h - 1)
                    for n in range(NCH):
                        last = dve.tensor_scalar(stat[:, h % 2, chunk(n)], banks[h % 2][n][:, :TC], 1.0 / P, SUBLN_EPS,
                                                 ALU.mult, ALU.add)
                    last.then_inc(taken, 1)
                    dve.wait_ge(taken, h + 1)
                    dve.reciprocal(stat[:, h % 2], stat[:, h % 2]).then_inc(inv, 1)
                    if h == 0:
                        dve.wait_ge(gain_ready, 1)
                    dve.wait_ge(rooted, h + 1)
                    dve.scalar_tensor_tensor(mixT[:, h], mixT[:, h], gain[:, 0:1], stat[:, h % 2],
                                             ALU.mult, ALU.mult).then_inc(read, 1)
                dve.wait_ge(summed, AH + 1)
                for n in range(NCH):
                    last = dve.tensor_scalar(mean[:, chunk(n)], banks[0][n][:, :TC], 1.0 / (BT * P), None, ALU.mult)
                last.then_inc(meaned, 1)
                dve.wait_ge(meaned, 1)
                dve.wait_ge(shifted, 2 * BT)
                for c in range(BT):
                    dve.tensor_tensor(mixT[:, AH + c], mixT[:, AH + c], mean[:], ALU.subtract).then_inc(centred, 1)
                dve.wait_ge(summed, AH + 1 + BT)
                dve.wait_ge(read, AH)
                for n in range(NCH):
                    last = dve.tensor_scalar(stat[:, 0, chunk(n)], banks[1][n][:, :TC], 1.0 / (BT * P), LN_EPS,
                                             ALU.mult, ALU.add)
                last.then_inc(taken, 1)
                dve.wait_ge(taken, AH + 1)
                dve.reciprocal(stat[:, 0], stat[:, 0]).then_inc(inv, 1)
                dve.wait_ge(rooted, AH + 1)
                for c in range(BT):
                    dve.tensor_tensor(mixT[:, AH + c], mixT[:, AH + c], stat[:, 0], ALU.mult).then_inc(read, 1)


def attention_layer(nc, hT, K, cst, vec, A, O):
    with Stage(nc, "a") as st:
        mixT = st.sb("mixT", [P, KD, T])
        glu = st.sb("glu", [P, BT, LEAD + T])
        glu_s = st.sb("glu_sample", [P, BT, NB, LEAD + NT])
        V = st.sb("values", [P, TP // P + 1, AH * P])
        lam = st.sb("lam", [P, 3])
        qkT = st.sb("qkT", [P, 2 * AH, T])
        uT = mixT
        uk = lambda k, n: uT[:, k, chunk(n)]
        rms_norm(nc, "nm0", hT, vec[:, VEC.at["mix"]][:, :KD], uT, K)
        gated_projection(nc, "gl", uk, A["w_glu"], BT, ACT.Sigmoid, glu, LEAD)
        with Stage(nc, "qk") as s2:
            trig, trig_in = s2.sb("trig", [P, 2 * T]), s2.sem("trig_in")
            with nc.Block() as block:
                @block.sync
                def _(sp):
                    sp.dma_start(trig[:], A["trig"]).then_inc(trig_in, 16)
                    sp.dma_start(O["conv_p"], glu[:, :, TP:TP + LEAD]).then_inc(trig_in, 16)
                    sp.wait_ge(trig_in, 32)

                @block.gpsimd
                def _(pool):
                    pool.memset(glu[:, :, 0:LEAD], 0.0)
            rotary_projection(nc, "rot", uT, A["w_qk"], trig, K, qkT, glu, vec)
        with Stage(nc, "vt") as s2:
            vT = s2.sb("vT", [P, AH, T])
            plain_projection(nc, "vp", uk, A["w_v"], AH, vT)
            keys_values_out(nc, qkT, vT, V, glu, glu_s, mixT[:, AH:, TP:], lam, vec, K, A, O)
        prompt_attention(nc, qkT, V, lam, mixT, K)
        sample_attention(nc, qkT, V, lam, mixT, K, cst, A)
        finish_mix(nc, mixT, glu, K, vec)
        add_projection(nc, "wo", lambda k, n: mixT[:, k, chunk(n)], KD, A["w_out"], hT)


LORA_W, LORA_A = slice(0, LW), slice(LW, 2 * LW)
G2 = LG - P
SIX = ("r", "w", "k", "v", "a", "g")


def shift_difference(nc, uT, xx, vec, O):
    with Stage(nc, "sh") as st:
        last = st.sb("last_rows", [P, KD, 1 + NB])
        copied, stored = st.sem("last_copied"), st.sem("stored")
        state = vec[:, VEC.at["shift"]].rearrange("p (k b) -> p k b", b=NB)
        first = uT[:, :, TP:].rearrange("p k (b t) -> p k b t", t=NT)
        firstx = xx[:, :, TP:].rearrange("p k (b t) -> p k b t", t=NT)
        plain = st.sem("inner_done")
        with nc.Block() as block:
            @block.vector
            def _(dve):
                dve.tensor_copy(last[:, :, 0:1], uT[:, :, TP - 1:TP]).then_inc(copied, 1)
                dve.tensor_copy(last[:, :, 1:], first[:, :, :, NT - 1]).then_inc(copied, 1)
                for k in range(KD):
                    dve.tensor_tensor(xx[:, k, 1:], uT[:, k, :T - 1], uT[:, k, 1:], ALU.subtract).then_inc(plain, 1)
                dve.tensor_scalar(xx[:, :, 0:1], uT[:, :, 0:1], -1.0, None, ALU.mult)
                dve.wait_ge(plain, KD)
                for k in range(KD):
                    dve.tensor_tensor(firstx[:, k, :, 0], state[:, k], first[:, k, :, 0], ALU.subtract)

            @block.sync
            def _(sp):
                sp.wait_ge(copied, 2)
                sp.dma_start(O["shift"], last[:]).then_inc(stored, 16)
                sp.wait_ge(stored, 16)


def mixed_projections(nc, uT, xx, vec, lora, lora_g2, A, scratch):
    with Dense(nc, "mp", KD) as st:
        xm = st.sb("mixed", [P, 2, KD, T])
        out = st.sb("out_tile", [P, 2, T])
        mixed, job_done = st.sem("mixed"), st.sem("job_done")
        stored = [st.sem(f"stored{s}") for s in range(2)]
        small_in, small_done = st.sem("lora_weights_loaded"), st.sem("lora_done")
        mu = vec[:, VEC.at["mu"]].rearrange("p (j k) -> p j k", k=KD)
        jobs = ("r", "k", "v", "w", "a", "g")
        w_lo, w_hi = st.slots[:, 0], st.slots[:, 1]
        wa1 = w_lo.rearrange("p (s k m) -> p s k m", s=2, k=KD)
        with nc.Block() as block:
            @block.vector
            def _(dve):
                for j, name in enumerate(jobs):
                    if j >= 2:
                        dve.wait_ge(job_done, j - 1)
                    for k in range(KD):
                        dve.scalar_tensor_tensor(xm[:, j % 2, k], xx[:, k], mu[:, SIX.index(name), k:k + 1],
                                                 uT[:, k], ALU.mult, ALU.add).then_inc(mixed, 1)

            @block.sync
            def _(sp):
                for s in range(2):
                    sp.dma_start(st.slots[:, s], A["w_rkv"][s]).then_inc(st.loaded[s], 16)
                with sp.Fori(1, 3 * KD // 2) as it:
                    for s in range(2):
                        sp.wait_ge(st.chunk_done, it * (2 * NCH) + (s - 1) * NCH)
                        sp.dma_start(st.slots[:, s], A["w_rkv"][ds(it * 2 + s, 1)][0]).then_inc(st.loaded[s], 16)
                sp.wait_ge(st.chunk_done, 3 * KD * NCH)
                sp.dma_start(w_lo, A["w_wa1"]).then_inc(small_in, 16)
                sp.dma_start(w_hi, A["w_g1"][0]).then_inc(small_in, 16)
                sp.wait_ge(small_done, 2 * NCH)
                sp.dma_start(w_lo[:, :KD * G2], A["w_g1b"]).then_inc(small_in, 16)

            @block.tensor
            def _(pe):
                for j in range(3):
                    pe.wait_ge(mixed, (j + 1) * KD)
                    with pe.Fori(0, KD // 2) as it:
                        for s in range(2):
                            pe.wait_ge(st.loaded[s], it * 16 + (16 + j * (KD // 2) * 16))
                            for n in range(NCH):
                                pe.wait_ge(st.bank_free[s], it * NCH + (n + 1 + j * (KD // 2) * NCH))
                                for k in range(KD):
                                    last = pe.matmul(st.banks[s * NCH + n][:, :TC], st.slots[:, s, k * P:(k + 1) * P],
                                                     xm[:, j % 2, k, chunk(n)], start=(k == 0), stop=(k == KD - 1))
                                last.then_inc(st.chunk_done, 1)
                    pe.wait_ge(st.chunk_done, (j + 1) * KD * NCH)
                    pe.sem_inc(job_done, 1)
                for s in range(2):
                    pe.wait_ge(st.bank_free[s], 3 * (KD // 2) * NCH + NCH)
                pe.wait_ge(small_in, 32)
                for j, rows in ((3, LORA_W), (4, LORA_A)):
                    pe.wait_ge(mixed, (j + 1) * KD)
                    for n in range(NCH):
                        for k in range(KD):
                            last = pe.matmul(st.banks[(j - 3) * NCH + n][rows, :TC], wa1[:, j - 3, k],
                                             xm[:, j % 2, k, chunk(n)], start=(k == 0), stop=(k == KD - 1))
                        last.then_inc(small_done, 1)
                    pe.wait_ge(small_done, (j - 2) * NCH)
                    pe.sem_inc(job_done, 1)
                pe.wait_ge(mixed, 6 * KD)
                pe.wait_ge(small_in, 48)
                for part in range(2):
                    for n in range(NCH):
                        pe.wait_ge(st.bank_free[part], 3 * (KD // 2) * NCH + NCH + n + 1)
                        for k in range(KD):
                            w = w_hi[:, k * P:(k + 1) * P] if part == 0 else w_lo[:, k * G2:(k + 1) * G2]
                            last = pe.matmul(st.banks[part * NCH + n][:P if part == 0 else G2, :TC], w,
                                             xm[:, 1, k, chunk(n)], start=(k == 0), stop=(k == KD - 1))
                        last.then_inc(small_done, 1)

            @block.scalar
            def _(act):
                for s in range(2):
                    act.sem_inc(st.bank_free[s], NCH)
                for s in range(2):
                    act.sem_inc(stored[s], 16)
                with act.Fori(0, 3 * KD // 2) as it:
                    for s in range(2):
                        act.wait_ge(stored[s], it * 16 + 16)
                        for n in range(NCH):
                            act.wait_ge(st.chunk_done, it * (2 * NCH) + s * NCH + n + 1)
                            act.activation(out[:, s, chunk(n)], st.banks[s * NCH + n][:, :TC],
                                           ACT.Copy).then_inc(st.bank_free[s], 1)
                        act.wait_ge(st.bank_free[s], it * NCH + 2 * NCH)
                        act.dma_start(scratch["rkv"][ds(it * 2 + s, 1)][0], out[:, s]).then_inc(stored[s], 16)
                for i, (rows, func) in enumerate(((LORA_W, ACT.Tanh), (LORA_A, ACT.Copy))):
                    for n in range(NCH):
                        act.wait_ge(small_done, i * NCH + n + 1)
                        act.activation(lora[rows, 0, chunk(n)], st.banks[i * NCH + n][rows, :TC],
                                       func).then_inc(st.bank_free[i], 1)
                for part, dst in enumerate((lora[:, 1], lora_g2[:])):
                    for n in range(NCH):
                        act.wait_ge(small_done, (2 + part) * NCH + n + 1)
                        act.activation(dst[:, chunk(n)], st.banks[part * NCH + n][:P if part == 0 else G2, :TC],
                                       ACT.Sigmoid)
                for s in range(2):
                    act.wait_ge(stored[s], 16 + 3 * KD // 2 * 16)


def prepare_chunks(nc, lora, el, K, vec, A, scratch):
    with Stage(nc, "pc") as st:
        keep = st.sb("keep", [P, T])
        rkv = st.sb("rkv", [P, 2, 3, T])
        w2 = st.sb("lora2", [P, 2, P])
        sg, a, cs, dif = (st.sb(n, [P, T]) for n in ("sig_w", "a", "cum", "cum_prev"))
        E, Ei, Ep = (st.sb(n, [P, T]) for n in ("decay", "decay_inv", "decay_prev"))
        sq, kk, t = (st.sb(n, [P, T]) for n in ("sq", "kk", "t"))
        outs = {n: st.sb("out_" + n, [P, 2, T]) for n in ("a", "b", "k", "r", "bonus")}
        omka = st.sb("one_minus_ka", [P, KD])
        banks = [st.bank(f"b{i}") for i in range(2 * NCH)]
        S = {n: st.sem(n) for n in (
            "loaded0", "loaded1", "keep_in", "lora_w", "lora_a", "sig", "a", "squared", "norm_sum", "rooted", "cum",
            "cum_prev", "E", "Ei", "Ep", "floor", "inv", "kk", "at", "m1", "bt", "t", "k2", "kt", "rt", "rk",
            "bonus_sum", "bonus", "el", "omka")}
        stored = [st.sem(f"stored{s}") for s in range(2)]
        col = lambda n: vec[:, VEC.at[n]]
        with nc.Block() as block:
            @block.sync
            def _(sp):
                sp.dma_start(keep[:], A["keep"]).then_inc(S["keep_in"], 16)

                def load(i, s):
                    for j in range(3):
                        sp.dma_start(rkv[:, s, j], scratch["rkv"][ds(i + j * KD, 1)][0]).then_inc(S[f"loaded{s}"], 16)
                    sp.dma_start(w2[:, s], A["w_wa2"][ds(i, 1)][0]).then_inc(S[f"loaded{s}"], 16)

                def store(i, s):
                    for n in ("kt", "at", "bt", "rt"):
                        sp.wait_ge(S[n], START + i + 1)
                    sp.wait_ge(S["bonus"], i * NCH + 3 * NCH)
                    for n in ("a", "b", "k", "r", "bonus"):
                        sp.dma_start(scratch[n][ds(i, 1)][0], outs[n][:, s]).then_inc(stored[s], 16)

                for s in range(2):
                    sp.sem_inc(stored[s], 16 * START)
                    load(s, s)
                with sp.Fori(0, KD // 2 - 1) as it:
                    for s in range(2):
                        store(it * 2 + s, s)
                        load(it * 2 + s + 2, s)
                for s in range(2):
                    store(KD - 2 + s, s)
                for s in range(2):
                    sp.wait_ge(stored[s], 16 * START + KD // 2 * 80)

            @block.tensor
            def _(pe):
                def lora_w(i, s, it):
                    pe.wait_ge(S[f"loaded{s}"], it * 64 + 64)
                    pe.wait_ge(S["floor"], START + i * NCH)
                    for n in range(NCH):
                        last = pe.matmul(banks[n][:, :TC], w2[LORA_W, s], lora[LORA_W, 0, chunk(n)],
                                         start=True, stop=True)
                    last.then_inc(S["lora_w"], 1)

                def tile(i, s, it, final=False):
                    pe.wait_ge(S["sig"], i * NCH + NCH)
                    pe.wait_ge(S["squared"], i + 1)
                    for n in range(NCH):
                        last = pe.matmul(banks[n][:, :TC], K.headones, sq[:, chunk(n)], start=True, stop=True)
                    last.then_inc(S["norm_sum"], 1)
                    pe.wait_ge(S["bonus"], i * NCH + 2 * NCH)
                    for n in range(NCH):
                        last = pe.matmul(banks[NCH + n][:, :TC], w2[LORA_A, s], lora[LORA_A, 0, chunk(n)],
                                         start=True, stop=True)
                    last.then_inc(S["lora_a"], 1)
                    if not final:
                        lora_w(i + 1, 1 - s, it + s)
                    pe.wait_ge(S["a"], i * NCH + NCH)
                    pe.wait_ge(S["rk"], i + 1)
                    for n in range(NCH):
                        last = pe.matmul(banks[NCH + n][:, :TC], K.headones, t[:, chunk(n)], start=True, stop=True)
                    last.then_inc(S["bonus_sum"], 1)

                lora_w(0, 0, 0)
                with pe.Fori(0, KD // 2 - 1) as it:
                    for s in range(2):
                        tile(it * 2 + s, s, it)
                for s in range(2):
                    tile(KD - 2 + s, s, KD // 2 - 1, final=(s == 1))

            @block.scalar
            def _(act):
                def begin(i, s, it):
                    act.wait_ge(S["lora_w"], i + 1)
                    act.wait_ge(S["cum_prev"], START + i)
                    for n in range(NCH):
                        act.activation(sg[:, chunk(n)], banks[n][:, :TC], ACT.Sigmoid,
                                       bias=col("w0")[:, ds(i, 1)]).then_inc(S["sig"], 1)
                    act.wait_ge(S["kk"], START + i)
                    act.wait_ge(S[f"loaded{s}"], it * 64 + 64)
                    act.activation(sq[:], rkv[:, s, 1], ACT.Square, scale=col("kk")[:, ds(i, 1)]).then_inc(S["squared"], 1)

                def tile(i):
                    act.wait_ge(S["norm_sum"], i + 1)
                    for n in range(NCH):
                        act.activation(sq[:, chunk(n)], banks[n][:, :TC], ACT.Sqrt).then_inc(S["floor"], 1)
                    act.wait_ge(S["floor"], START + i * NCH + NCH)
                    act.sem_inc(S["rooted"], 1)
                    act.wait_ge(S["lora_a"], i + 1)
                    act.wait_ge(S["t"], START + i)
                    act.wait_ge(S["m1"], START + i)
                    for n in range(NCH):
                        act.activation(a[:, chunk(n)], banks[NCH + n][:, :TC], ACT.Sigmoid,
                                       bias=col("a0")[:, ds(i, 1)]).then_inc(S["a"], 1)
                    act.wait_ge(S["cum"], i + 1)
                    act.wait_ge(S["rt"], START + i)
                    act.wait_ge(S["el"], START + i * 2)
                    act.activation(E[:], cs[:], ACT.Exp, scale=-DECAY).then_inc(S["E"], 1)
                    act.wait_ge(S["bt"], START + i)
                    act.wait_ge(S["kt"], START + i)
                    act.activation(Ei[:], cs[:], ACT.Exp, scale=DECAY).then_inc(S["Ei"], 1)
                    act.wait_ge(S["cum_prev"], START + i + 1)
                    act.wait_ge(S["at"], START + i)
                    act.activation(Ep[:], dif[:], ACT.Exp, scale=-DECAY).then_inc(S["Ep"], 1)

                for n in ("floor", "Ep"):
                    act.sem_inc(S[n], START)
                begin(0, 0, 0)
                with act.Fori(0, KD // 2 - 1) as it:
                    for s in range(2):
                        tile(it * 2 + s)
                        begin(it * 2 + s + 1, 1 - s, it + s)
                tile(KD - 2)
                begin(KD - 1, 1, KD // 2 - 1)
                tile(KD - 1)

            @block.vector
            def _(dve):
                dve.sem_inc(S["bonus"], 2 * NCH)
                dve.tensor_scalar(omka[:], col("ka"), -1.0, 1.0, ALU.mult, ALU.add).then_inc(S["omka"], 1)
                dve.wait_ge(S["omka"], 1)
                dve.wait_ge(S["keep_in"], 16)
                for n in ("kk", "t", "el", "kt", "at"):
                    dve.sem_inc(S[n], START)
                with dve.Fori(0, KD // 2) as it:
                    for s in range(2):
                        i = it * 2 + s
                        r, k, v = (rkv[:, s, j] for j in range(3))
                        dve.wait_ge(S["Ep"], START + i)
                        dve.wait_ge(S["sig"], i * NCH + NCH)
                        dve.tensor_tensor_scan(cs[:], keep[:], sg[:], 0.0, ALU.mult, ALU.add).then_inc(S["cum"], 1)
                        dve.wait_ge(S["rooted"], i + 1)
                        dve.tensor_scalar(sq[:], sq[:], 1e-12, None, ALU.max).then_inc(S["inv"], 1)
                        dve.wait_ge(S["inv"], i * 2 + 1)
                        dve.reciprocal(sq[:], sq[:]).then_inc(S["inv"], 1)
                        dve.wait_ge(S["a"], i * NCH + NCH)
                        dve.tensor_scalar(t[:], a[:], col("ka")[:, ds(i, 1)], omka[:, ds(i, 1)],
                                          ALU.mult, ALU.add).then_inc(S["t"], 1)
                        dve.wait_ge(stored[s], 16 * START + it * 80)
                        dve.wait_ge(S["t"], START + i + 1)
                        dve.tensor_tensor(t[:], k, t[:], ALU.mult).then_inc(S["k2"], 1)
                        dve.wait_ge(S["inv"], i * 2 + 2)
                        dve.wait_ge(S["at"], START + i)
                        dve.wait_ge(S["m1"], START + i)
                        dve.scalar_tensor_tensor(kk[:], k, col("kk")[:, ds(i, 1)], sq[:], ALU.mult, ALU.mult).then_inc(S["kk"], 1)
                        dve.wait_ge(S["Ei"], i + 1)
                        dve.wait_ge(S["k2"], i + 1)
                        dve.tensor_tensor(outs["k"][:, s], t[:], Ei[:], ALU.mult).then_inc(S["kt"], 1)
                        dve.scalar_tensor_tensor(t[:], r, col("rk")[:, ds(i, 1)], t[:], ALU.mult, ALU.mult).then_inc(S["rk"], 1)
                        dve.wait_ge(S["Ep"], START + i + 1)
                        dve.wait_ge(S["kk"], START + i + 1)
                        dve.scalar_tensor_tensor(outs["a"][:, s], kk[:], -1.0, Ep[:], ALU.mult, ALU.mult).then_inc(S["at"], 1)
                        dve.tensor_copy(el[:, ds(i, 1), 0:NC][:, 0], E[:, CL - 1:TP:CL]).then_inc(S["el"], 1)
                        dve.tensor_copy(el[:, ds(i, 1), NC:][:, 0], E[:, TP + NT - 1::NT]).then_inc(S["el"], 1)
                        dve.wait_ge(S["bonus_sum"], i + 1)
                        for n in range(NCH):
                            dve.tensor_tensor(outs["bonus"][:, s, chunk(n)], banks[NCH + n][:, :TC], v[:, chunk(n)],
                                              ALU.mult).then_inc(S["bonus"], 1)

            @block.gpsimd
            def _(pool):
                for n in ("cum_prev", "m1", "rt", "bt"):
                    pool.sem_inc(S[n], START)
                with pool.Fori(0, KD // 2) as it:
                    for s in range(2):
                        i = it * 2 + s
                        pool.wait_ge(S["Ep"], START + i)
                        pool.wait_ge(S["cum"], i + 1)
                        pool.tensor_tensor(dif[:], cs[:], sg[:], ALU.subtract).then_inc(S["cum_prev"], 1)
                        pool.wait_ge(stored[s], 16 * START + it * 80)
                        pool.wait_ge(S["E"], i + 1)
                        pool.tensor_tensor(outs["r"][:, s], rkv[:, s, 0], E[:], ALU.mult).then_inc(S["rt"], 1)
                        pool.wait_ge(S["kk"], START + i + 1)
                        pool.tensor_tensor(outs["b"][:, s], kk[:], a[:], ALU.mult).then_inc(S["m1"], 1)
                        pool.wait_ge(S["m1"], START + i + 1)
                        pool.wait_ge(S["Ei"], i + 1)
                        pool.tensor_tensor(outs["b"][:, s], outs["b"][:, s], Ei[:], ALU.mult).then_inc(S["bt"], 1)


PRODUCTS = ("P", "Q", "K", "A", "V", "bT", "kT", "D2", "D2T", "X1", "D4", "D4T", "X2", "D8", "X3",
            "FT", "X", "Z1", "Z2", "Z3", "W", "U", "Y", "dS")
BY_DVE = ("D", "E", "DT", "X0", "K", "A", "X1", "X2", "X3", "Z1", "Z2", "Z3", "S1", "S2")
BY_ACT = ("V", "bT", "kT", "D2", "D2T", "D4", "D4T", "D8", "FT", "X", "W", "U", "Y")
GP = PAIRS // 2


class Group:

    def __init__(self, st, g, slots):
        self.g = g
        wide = ("a", "b", "k", "v")
        self.inp = {n: st.sb(f"{n}{g}", [P, slots, GP, P]) for n in wide}
        self.r = st.sb(f"r{g}", [P, slots, GP, CL])
        names = ("V", "bT", "kT", "D2", "D2T", "D4", "D4T", "D8", "FT", "X", "W", "U")
        self.copy = {n: st.sb(f"{n}_{g}", [P, GP, P]) for n in names}
        (self.V, self.bT, self.kT, self.D2, self.D2T, self.D4, self.D4T, self.D8, self.FT, self.X, self.W,
         self.U) = (self.copy[n] for n in names)
        self.D, self.E, self.DT, self.XT, self.K, self.A, self.Z, self.S = (
            st.sb(f"{n}_{g}", [P, GP, P]) for n in ("D", "E", "DT", "XT", "K", "A", "Z", "S"))
        self.bank = [st.bank(f"bank{g}{i}") for i in range(4)]
        self.loaded = [st.sem(f"loaded{g}{s}") for s in range(slots)]
        self.products, self.dve, self.act = st.sem(f"products{g}"), st.sem(f"by_vector{g}"), st.sem(f"by_scalar{g}")


def product(c, name):
    return c * len(PRODUCTS) + (PRODUCTS.index(name) + 1 + START)


def vec_step(c, name):
    return c * len(BY_DVE) + (BY_DVE.index(name) + 1 + START)


def act_step(c, name):
    return c * len(BY_ACT) + (BY_ACT.index(name) + 1 + START)


def load_chunk(sp, B, slot, scratch, start):
    pairs = slice(B.g * GP, (B.g + 1) * GP)
    for n in ("b", "a", "k", "v"):
        src = scratch["v" if n == "v" else n]
        for h in range(2):
            rows = slice(h * DH, (h + 1) * DH)
            sp.dma_start(B.inp[n][rows, slot, :, h * CL:(h + 1) * CL],
                         src[pairs, rows, start].rearrange("q p t -> p q t")).then_inc(B.loaded[slot], 16)
    sp.dma_start(B.r[:, slot], scratch["r"][pairs, :, start].rearrange("q p t -> p q t")).then_inc(B.loaded[slot], 16)


def pairs_product(pe, bank, lhsT, rhs):
    for p in range(GP):
        last = pe.matmul(bank[:, p * P:(p + 1) * P], lhsT[:, p], rhs[:, p], start=True, stop=True)
    return last


def tensor_inner(pe, groups, slot, c, K):
    for B in groups:
        pe.wait_ge(B.act, c * len(BY_ACT) + START)
        pairs_product(pe, B.bank[0], B.inp["b"][:, slot], B.inp["a"][:, slot]).then_inc(B.products, 1)
    for B in groups:
        pairs_product(pe, B.bank[1], B.inp["a"][:, slot], B.inp["b"][:, slot]).then_inc(B.products, 1)
    for B in groups:
        pairs_product(pe, B.bank[2], B.inp["k"][:, slot], B.inp["a"][:, slot]).then_inc(B.products, 1)
    for B in groups:
        pe.wait_ge(B.dve, c * len(BY_DVE) + START)
        for p in range(GP):
            pe.matmul(B.bank[3][:, p * P:p * P + CL], B.inp["b"][:, slot, p], B.r[:, slot, p], start=True, stop=True)
            last = pe.matmul(B.bank[3][:, p * P + CL:(p + 1) * P], B.inp["k"][:, slot, p], B.r[:, slot, p],
                             start=True, stop=True)
        last.then_inc(B.products, 1)
    for name, bank, freed in (("v", 0, "E"), ("b", 1, "DT"), ("k", 2, "K")):
        for B in groups:
            pe.wait_ge(B.dve, vec_step(c, freed))
            for p in range(GP):
                last = pe.transpose(B.bank[bank][:, p * P:(p + 1) * P], B.inp[name][:, slot, p], K.ident)
            last.then_inc(B.products, 1)
    for B in groups:
        pe.wait_ge(B.dve, vec_step(c, "A"))
        pairs_product(pe, B.bank[3], B.DT, B.D).then_inc(B.products, 1)
    for B in groups:
        pe.wait_ge(B.act, act_step(c, "V"))
        pairs_product(pe, B.bank[0], B.D, B.DT).then_inc(B.products, 1)
    for B in groups:
        pe.wait_ge(B.act, act_step(c, "D2"))
        pairs_product(pe, B.bank[1], B.D2, B.XT).then_inc(B.products, 1)
    for B in groups:
        pe.wait_ge(B.act, act_step(c, "D2T"))
        pairs_product(pe, B.bank[2], B.D2T, B.D2).then_inc(B.products, 1)
    for B in groups:
        pairs_product(pe, B.bank[3], B.D2, B.D2T).then_inc(B.products, 1)
    for B in groups:
        pe.wait_ge(B.act, act_step(c, "D4"))
        pe.wait_ge(B.dve, vec_step(c, "X1"))
        pairs_product(pe, B.bank[0], B.D4, B.XT).then_inc(B.products, 1)
    for B in groups:
        pe.wait_ge(B.act, act_step(c, "D4T"))
        pairs_product(pe, B.bank[1], B.D4T, B.D4).then_inc(B.products, 1)
    for B in groups:
        pe.wait_ge(B.act, act_step(c, "D8"))
        pe.wait_ge(B.dve, vec_step(c, "X2"))
        pairs_product(pe, B.bank[2], B.D8, B.XT).then_inc(B.products, 1)
    for B in groups:
        pe.wait_ge(B.dve, vec_step(c, "X3"))
        pairs_product(pe, B.bank[3], B.E, B.XT).then_inc(B.products, 1)
    for B in groups:
        for p in range(GP):
            last = pe.transpose(B.bank[0][:, p * P:(p + 1) * P], B.XT[:, p], K.ident)
        last.then_inc(B.products, 1)
    for B in groups:
        pe.wait_ge(B.act, act_step(c, "X"))
        pairs_product(pe, B.bank[1], B.FT, B.X).then_inc(B.products, 1)
    for bank, need in ((2, "Z1"), (3, "Z2")):
        for B in groups:
            pe.wait_ge(B.dve, vec_step(c, need))
            pairs_product(pe, B.bank[bank], B.FT, B.Z).then_inc(B.products, 1)


def vector_inner(dve, groups, c, cst, tag):
    mask = {n: cst[:, CONST.at[f"{n}_{tag}"]] for n in ("d", "e", "dT", "a", "q")}
    wide = lambda x: x.unsqueeze(1).broadcast_to([P, GP, P])
    tile = lambda x: x[:, :].rearrange("p (q t) -> p q t", t=P)
    ident = cst[:, CONST.at["ident"]]
    for B in groups:
        dve.wait_ge(B.products, product(c, "P"))
        dve.tensor_tensor(B.D[:], tile(B.bank[0]), wide(mask["d"]), ALU.mult).then_inc(B.dve, 1)
        dve.tensor_tensor(B.E[:], tile(B.bank[0]), wide(mask["e"]), ALU.mult).then_inc(B.dve, 1)
    for B in groups:
        dve.wait_ge(B.products, product(c, "Q"))
        dve.tensor_tensor(B.DT[:], tile(B.bank[1]), wide(mask["dT"]), ALU.mult).then_inc(B.dve, 1)
    for B in groups:
        dve.wait_ge(B.dve, vec_step(c, "DT"))
        dve.tensor_tensor(B.XT[:], B.DT[:], wide(ident), ALU.add).then_inc(B.dve, 1)
    for B in groups:
        dve.wait_ge(B.products, product(c, "K"))
        dve.tensor_tensor(B.K[:], tile(B.bank[2]), wide(mask["a"]), ALU.mult).then_inc(B.dve, 1)
    for B in groups:
        dve.wait_ge(B.products, product(c, "A"))
        dve.tensor_tensor(B.A[:].rearrange("p q (w t) -> p (q w) t", w=2),
                          B.bank[3][:].rearrange("p (x t) -> p x t", t=CL),
                          mask["q"].unsqueeze(1).broadcast_to([P, 2 * GP, CL]), ALU.mult).then_inc(B.dve, 1)
    for name, bank in (("X1", 1), ("X2", 0), ("X3", 2)):
        for B in groups:
            dve.wait_ge(B.products, product(c, name))
            dve.tensor_tensor(B.XT[:], tile(B.bank[bank]), B.XT[:], ALU.add).then_inc(B.dve, 1)
    for name, bank in (("Z1", 1), ("Z2", 2), ("Z3", 3)):
        for B in groups:
            dve.wait_ge(B.products, product(c, name))
            dve.tensor_tensor(B.Z[:], tile(B.bank[bank]), B.X[:], ALU.add).then_inc(B.dve, 1)


def scalar_inner(act, groups, c):
    for name, bank in (("V", 0), ("bT", 1), ("kT", 2), ("D2", 3), ("D2T", 0), ("D4", 2), ("D4T", 3), ("D8", 1),
                       ("FT", 3), ("X", 0)):
        for B in groups:
            act.wait_ge(B.products, product(c, name))
            act.activation(B.copy[name][:].rearrange("p q t -> p (q t)"), B.bank[bank][:], ACT.Copy).then_inc(B.act, 1)


def prompt_chunks(nc, el, yT, K, cst, scratch, O):
    with Stage(nc, "ch") as st:
        groups = [Group(st, g, 2) for g in range(2)]
        zeroed, stored = st.sem("zeroed"), st.sem("stored")
        LOADS = 9 * 16
        with nc.Block() as block:
            @block.gpsimd
            def _(pool):
                for B in groups:
                    for n in ("a", "b", "k", "v"):
                        pool.memset(B.inp[n][:], 0.0).then_inc(zeroed, 1)
                    pool.memset(B.S[:], 0.0).then_inc(zeroed, 1)

            @block.sync
            def _(sp):
                sp.wait_ge(zeroed, 10)
                for slot in range(2):
                    for B in groups:
                        load_chunk(sp, B, slot, scratch, slice(slot * CL, (slot + 1) * CL))
                with sp.Fori(1, NC // 2) as it:
                    for slot in range(2):
                        for B in groups:
                            sp.wait_ge(B.products, it * (2 * len(PRODUCTS)) + ((slot - 1) * len(PRODUCTS) + START))
                            load_chunk(sp, B, slot, scratch, ds(it * (2 * CL) + slot * CL, CL))
                for B in groups:
                    sp.wait_ge(B.dve, NC * len(BY_DVE) + START)
                    for h in range(2):
                        rows = slice(h * DH, (h + 1) * DH)
                        sp.dma_start(O["wkv_p"][rows, B.g * GP:(B.g + 1) * GP],
                                     B.S[rows, :, h * DH:(h + 1) * DH]).then_inc(stored, 16)
                sp.wait_ge(stored, 64)

            @block.tensor
            def _(pe):
                for B in groups:
                    pe.sem_inc(B.products, START)
                pe.wait_ge(zeroed, 10)
                with pe.Fori(0, NC // 2) as it:
                    for slot in range(2):
                        c = it * 2 + slot
                        for B in groups:
                            pe.wait_ge(B.loaded[slot], it * LOADS + LOADS)
                        tensor_inner(pe, groups, slot, c, K)
                        for B in groups:
                            for p in range(GP):
                                o = B.bank[0][:, p * P:(p + 1) * P]
                                pe.matmul(o, B.inp["a"][:, slot, p], B.S[:, p], start=True, stop=False)
                                last = pe.matmul(o, B.K[:, p], B.V[:, p], start=False, stop=True)
                            last.then_inc(B.products, 1)
                        for B in groups:
                            pe.wait_ge(B.dve, vec_step(c, "Z3"))
                            pe.wait_ge(B.act, act_step(c, "W"))
                            pairs_product(pe, B.bank[1], B.Z, B.W).then_inc(B.products, 1)
                        for B in groups:
                            pe.wait_ge(B.act, act_step(c, "U"))
                            for p in range(GP):
                                o = B.bank[2][:, p * CL:(p + 1) * CL]
                                pe.matmul(o, B.S[:, p], B.r[:, slot, p], start=True, stop=False)
                                pe.matmul(o, B.U[:, p], B.A[:, p, :CL], start=False, stop=False)
                                last = pe.matmul(o, B.V[:, p], B.A[:, p, CL:], start=False, stop=True)
                            last.then_inc(B.products, 1)
                        for B in groups:
                            for p in range(GP):
                                o = B.bank[3][:, p * P:(p + 1) * P]
                                pe.matmul(o, B.bT[:, p], B.U[:, p], start=True, stop=False)
                                last = pe.matmul(o, B.kT[:, p], B.V[:, p], start=False, stop=True)
                            last.then_inc(B.products, 1)

            @block.scalar
            def _(act):
                for B in groups:
                    act.sem_inc(B.act, START)
                with act.Fori(0, NC // 2) as it:
                    for slot in range(2):
                        c = it * 2 + slot
                        scalar_inner(act, groups, c)
                        for B in groups:
                            act.wait_ge(B.products, product(c, "W"))
                            act.activation(B.W[:].rearrange("p q t -> p (q t)"), B.bank[0][:], ACT.Copy).then_inc(B.act, 1)
                        for B in groups:
                            act.wait_ge(B.products, product(c, "U"))
                            act.activation(B.U[:].rearrange("p q t -> p (q t)"), B.bank[1][:], ACT.Copy).then_inc(B.act, 1)
                        for B in groups:
                            act.wait_ge(B.products, product(c, "Y"))
                            act.activation(yT[:, B.g * GP:(B.g + 1) * GP, ds(it * (2 * CL) + slot * CL, CL)],
                                           B.bank[2][:, :GP * CL].rearrange("p (q t) -> p q t", t=CL),
                                           ACT.Copy).then_inc(B.act, 1)

            @block.vector
            def _(dve):
                for B in groups:
                    dve.sem_inc(B.dve, START)
                with dve.Fori(0, NC // 2) as it:
                    for slot in range(2):
                        c = it * 2 + slot
                        vector_inner(dve, groups, c, cst, "p")
                        for B in groups:
                            dve.wait_ge(B.products, product(c, "dS"))
                            dve.tensor_tensor(B.S[:], B.bank[3][:].rearrange("p (q t) -> p q t", t=P), B.S[:],
                                              ALU.add).then_inc(B.dve, 1)
                            dve.wait_ge(B.dve, vec_step(c, "S1"))
                            decay = el[:, B.g * GP:(B.g + 1) * GP, ds(c, 1)]
                            dve.tensor_tensor(B.S[:], B.S[:], decay.broadcast_to([P, GP, P]), ALU.mult).then_inc(B.dve, 1)


def sample_chunk(nc, el, yT, K, cst, A, scratch, O):
    with Stage(nc, "sc") as st:
        groups = [Group(st, g, 1) for g in range(2)]
        zeroed, loaded, stored = st.sem("zeroed"), [st.sem(f"state_loaded{i}") for i in range(2)], st.sem("stored")
        S = st.sb("states", [P, 2, NB, P])
        Sn = st.sb("new_states", [P, NB, P])
        WT, W, U = (st.sb(n, [P, P]) for n in ("WT", "W1", "U1"))
        Um, Vm = st.sb("U_rows", [P, NB, P]), st.sb("V_rows", [P, NB, P])
        names = ("WTp", "WTc", "Wp", "Wc", "Up", "Uc", "Um", "Vm", "Yp", "Yc", "dS", "S1", "S2")
        q_ = {n: st.sem("q_" + n) for n in names}
        brow = cst[:, CONST.at["brow"]].unsqueeze(2).broadcast_to([P, NB, P])
        with nc.Block() as block:
            @block.gpsimd
            def _(pool):
                for B in groups:
                    for n in ("a", "b", "k", "v"):
                        pool.memset(B.inp[n][:], 0.0).then_inc(zeroed, 1)
                    pool.memset(B.r[:], 0.0).then_inc(zeroed, 1)
                pool.memset(S[:], 0.0).then_inc(zeroed, 1)
                pool.memset(WT[:], 0.0).then_inc(zeroed, 1)

            def store(sp, q):
                sp.wait_ge(q_["S2"], 2 * (q + 1))
                for h in range(2):
                    rows = slice(h * DH, (h + 1) * DH)
                    sp.dma_start(O["wkv_s"][q, rows], Sn[rows, :, h * DH:(h + 1) * DH]).then_inc(stored, 16)

            @block.sync
            def _(sp):
                sp.wait_ge(zeroed, 12)
                for B in groups:
                    pairs = slice(B.g * GP, (B.g + 1) * GP)
                    for n in ("b", "a", "k", "v"):
                        for h in range(2):
                            rows = slice(h * DH, (h + 1) * DH)
                            sp.dma_start(B.inp[n][rows, 0, :, h * CL:h * CL + TS],
                                         scratch[n][pairs, rows, TP:].rearrange("q p t -> p q t")).then_inc(B.loaded[0], 16)
                    sp.dma_start(B.r[:, 0, :, :TS], scratch["r"][pairs, :, TP:].rearrange("q p t -> p q t")
                                 ).then_inc(B.loaded[0], 16)
                for q in range(PAIRS):
                    if q >= 2:
                        sp.wait_ge(q_["S1"], (q - 1) * 2)
                        sp.wait_ge(q_["dS"], q - 1)
                    for h in range(2):
                        rows = slice(h * DH, (h + 1) * DH)
                        sp.dma_start(S[rows, q % 2, :, h * DH:(h + 1) * DH], A["state_wkv"][q, rows]).then_inc(loaded[q % 2], 16)
                    if q >= 1:
                        store(sp, q - 1)
                store(sp, PAIRS - 1)
                sp.wait_ge(stored, PAIRS * 32)

            @block.tensor
            def _(pe):
                for B in groups:
                    pe.sem_inc(B.products, START)
                pe.wait_ge(zeroed, 12)
                for B in groups:
                    pe.wait_ge(B.loaded[0], 9 * 16)
                tensor_inner(pe, groups, 0, 0, K)
                for B in groups:
                    pe.wait_ge(B.dve, vec_step(0, "Z3"))
                bank = groups[0].bank + groups[1].bank
                for q in range(PAIRS):
                    B, p = groups[q // GP], q % GP
                    Sq = S[:, q % 2]
                    pe.wait_ge(loaded[q % 2], 32 * (q // 2 + 1))
                    if q:
                        pe.wait_ge(q_["WTc"], q)
                    a = B.inp["a"][:, 0, p].rearrange("p (h s) -> p h s", h=2)
                    o = bank[0][:, :P].rearrange("p (h s) -> p h s", h=2)
                    for b in range(NB):
                        cols = slice(b * NT, (b + 1) * NT)
                        last = pe.matmul(o[:, :, cols], Sq[:, b], a[:, :, cols], start=True, stop=True)
                    last.then_inc(q_["WTp"], 1)
                    pe.wait_ge(q_["WTc"], q + 1)
                    pe.matmul(bank[1][:, :P], WT[:], K.ident, start=True, stop=False)
                    pe.matmul(bank[1][:, :P], B.K[:, p], B.V[:, p], start=False, stop=True).then_inc(q_["Wp"], 1)
                    pe.wait_ge(q_["Wc"], q + 1)
                    if q:
                        pe.wait_ge(q_["Um"], q)
                    pe.matmul(bank[2][:, :P], B.Z[:, p], W[:], start=True, stop=True).then_inc(q_["Up"], 1)
                    pe.wait_ge(q_["Uc"], q + 1)
                    if q:
                        pe.wait_ge(q_["Yc"], q)
                    y = bank[3][:, :TS]
                    pe.matmul(y, U[:], B.A[:, p, :TS], start=True, stop=False)
                    pe.matmul(y, B.V[:, p], B.A[:, p, CL:CL + TS], start=False, stop=False)
                    for b in range(NB):
                        cols = slice(b * NT, (b + 1) * NT)
                        last = pe.matmul(bank[3][:, cols], Sq[:, b], B.r[:, 0, p, cols], start=False, stop=(b == NB - 1))
                    last.then_inc(q_["Yp"], 1)
                    pe.wait_ge(q_["Um"], q + 1)
                    pe.wait_ge(q_["Vm"], q + 1)
                    if q:
                        pe.wait_ge(q_["S1"], 2 * q)
                    for half in range(2):
                        bs = slice(half * 4, half * 4 + 4)
                        o = bank[4 + half][:]
                        pe.matmul(o, B.bT[:, p], Um[:, bs], start=True, stop=False)
                        last = pe.matmul(o, B.kT[:, p], Vm[:, bs], start=False, stop=True)
                    last.then_inc(q_["dS"], 1)

            @block.scalar
            def _(act):
                for B in groups:
                    act.sem_inc(B.act, START)
                scalar_inner(act, groups, 0)
                bank = groups[0].bank + groups[1].bank
                for q in range(PAIRS):
                    act.wait_ge(q_["WTp"], q + 1)
                    act.activation(WT[:].rearrange("p (h s) -> p h s", h=2)[:, :, :TS],
                                   bank[0][:, :P].rearrange("p (h s) -> p h s", h=2)[:, :, :TS], ACT.Copy).then_inc(q_["WTc"], 1)
                    act.wait_ge(q_["Wp"], q + 1)
                    act.activation(W[:], bank[1][:, :P], ACT.Copy).then_inc(q_["Wc"], 1)
                    act.wait_ge(q_["Up"], q + 1)
                    act.activation(U[:], bank[2][:, :P], ACT.Copy).then_inc(q_["Uc"], 1)
                    act.wait_ge(q_["Yp"], q + 1)
                    act.activation(yT[:, q, TP:], bank[3][:, :TS], ACT.Copy).then_inc(q_["Yc"], 1)

            @block.vector
            def _(dve):
                for B in groups:
                    dve.sem_inc(B.dve, START)
                vector_inner(dve, groups, 0, cst, "s")
                bank = groups[0].bank + groups[1].bank
                for B in groups:
                    dve.wait_ge(B.act, act_step(0, "X"))
                for q in range(PAIRS):
                    B, p = groups[q // GP], q % GP
                    if q:
                        dve.wait_ge(q_["dS"], q)
                    dve.tensor_tensor(Vm[:], B.V[:, p].unsqueeze(1).broadcast_to([P, NB, P]), brow,
                                      ALU.mult).then_inc(q_["Vm"], 1)
                    dve.wait_ge(q_["Uc"], q + 1)
                    dve.tensor_tensor(Um[:], U[:].unsqueeze(1).broadcast_to([P, NB, P]), brow,
                                      ALU.mult).then_inc(q_["Um"], 1)
                    dve.wait_ge(q_["dS"], q + 1)
                    if q:
                        dve.wait_ge(stored, 32 * q)
                    for half in range(2):
                        bs = slice(half * 4, half * 4 + 4)
                        dve.tensor_tensor(Sn[:, bs], bank[4 + half][:].rearrange("p (b t) -> p b t", t=P),
                                          S[:, q % 2, bs], ALU.add).then_inc(q_["S1"], 1)
                    dve.wait_ge(q_["S1"], 2 * (q + 1))
                    for half in range(2):
                        bs = slice(half * 4, half * 4 + 4)
                        decay = el[:, q, NC + half * 4:NC + half * 4 + 4].unsqueeze(2)
                        dve.tensor_tensor(Sn[:, bs], Sn[:, bs], decay.broadcast_to([P, 4, P]), ALU.mult).then_inc(q_["S2"], 1)


def finish_heads(nc, yT, lora, lora_g2, K, vec, A, scratch):
    with Stage(nc, "fh") as st:
        bonus = st.sb("bonus", [P, 2, T])
        g2 = st.sb("gate2", [P, 2, 2, P])
        d, sq, stat = st.sb("centred", [P, 2, T]), st.sb("sq", [P, 2, T]), st.sb("stat", [P, T])
        banks = [st.bank(f"b{i}") for i in range(2 * NCH)]
        q_ = {n: st.sem(n) for n in ("mean_sum", "centred", "sq", "var_sum", "var", "inv", "root", "n1", "n2",
                                     "gate", "gated")}
        loaded = [st.sem(f"loaded{s}") for s in range(2)]
        col = lambda n: vec[:, VEC.at[n]]
        with nc.Block() as block:
            @block.sync
            def _(sp):
                with sp.Fori(0, KD // 2) as it:
                    for s in range(2):
                        i = it * 2 + s
                        sp.wait_ge(q_["gated"], i * NCH + NCH)
                        sp.dma_start(bonus[:, s], scratch["bonus"][ds(i, 1)][0]).then_inc(loaded[s], 16)
                        sp.dma_start(g2[:, s, 0], A["w_g2"][ds(i, 1)][0]).then_inc(loaded[s], 16)
                        sp.dma_start(g2[:G2, s, 1], A["w_g2b"][ds(i, 1)][0]).then_inc(loaded[s], 16)

            @block.tensor
            def _(pe):
                def mean(i):
                    pe.wait_ge(q_["centred"], START + i * NCH)
                    row = yT[:, ds(i, 1)]
                    for n in range(NCH):
                        last = pe.matmul(banks[n][:, :TC], K.headones, row[:, 0, chunk(n)], start=True, stop=True)
                    last.then_inc(q_["mean_sum"], 1)

                def variance_and_gate(i, s, it):
                    pe.wait_ge(q_["sq"], i + 1)
                    pe.wait_ge(q_["gated"], i * NCH + 2 * NCH)
                    for n in range(NCH):
                        last = pe.matmul(banks[NCH + n][:, :TC], K.headones, sq[:, s, chunk(n)], start=True, stop=True)
                    last.then_inc(q_["var_sum"], 1)
                    pe.wait_ge(loaded[s], it * 48 + 48)
                    pe.wait_ge(q_["var"], (i + 1) * NCH)
                    for n in range(NCH):
                        pe.matmul(banks[NCH + n][:, :TC], g2[:, s, 0], lora[:, 1, chunk(n)], start=True, stop=False)
                        last = pe.matmul(banks[NCH + n][:, :TC], g2[:G2, s, 1], lora_g2[:, chunk(n)], start=False, stop=True)
                    last.then_inc(q_["gate"], 1)

                mean(0)
                with pe.Fori(0, KD // 2 - 1) as it:
                    for s in range(2):
                        mean(it * 2 + s + 1)
                        variance_and_gate(it * 2 + s, s, it)
                mean(KD - 1)
                for s in range(2):
                    variance_and_gate(KD - 2 + s, s, KD // 2 - 1)

            @block.scalar
            def _(act):
                def square(i, s):
                    act.wait_ge(q_["centred"], START + (i + 1) * NCH)
                    act.activation(sq[:, s], d[:, s], ACT.Square).then_inc(q_["sq"], 1)

                def root(i):
                    act.wait_ge(q_["inv"], i + 1)
                    act.activation(stat[:], stat[:], ACT.Sqrt).then_inc(q_["root"], 1)

                square(0, 0)
                with act.Fori(0, KD // 2 - 1) as it:
                    for s in range(2):
                        square(it * 2 + s + 1, 1 - s)
                        root(it * 2 + s)
                square(KD - 1, 1)
                for s in range(2):
                    root(KD - 2 + s)

            @block.vector
            def _(dve):
                def centre(i, s):
                    dve.wait_ge(q_["mean_sum"], i + 1)
                    dve.wait_ge(q_["gated"], (i + 1) * NCH)
                    row = yT[:, ds(i, 1)]
                    for n in range(NCH):
                        dve.scalar_tensor_tensor(d[:, s, chunk(n)], banks[n][:, :TC], -1.0 / DH, row[:, 0, chunk(n)],
                                                 ALU.mult, ALU.add).then_inc(q_["centred"], 1)

                def norm(i, s, it):
                    row = yT[:, ds(i, 1)]
                    dve.wait_ge(q_["var_sum"], i + 1)
                    for n in range(NCH):
                        dve.tensor_scalar(stat[:, chunk(n)], banks[NCH + n][:, :TC], 1.0 / DH, GN_EPS,
                                          ALU.mult, ALU.add).then_inc(q_["var"], 1)
                    dve.wait_ge(q_["var"], (i + 1) * NCH)
                    dve.reciprocal(stat[:], stat[:]).then_inc(q_["inv"], 1)
                    dve.wait_ge(q_["root"], i + 1)
                    dve.scalar_tensor_tensor(d[:, s], d[:, s], col("lnx_g")[:, ds(i, 1)], stat[:],
                                             ALU.mult, ALU.mult).then_inc(q_["n1"], 1)
                    dve.wait_ge(loaded[s], it * 48 + 48)
                    dve.wait_ge(q_["n1"], i + 1)
                    dve.scalar_tensor_tensor(d[:, s], d[:, s], col("lnx_b")[:, ds(i, 1)], bonus[:, s],
                                             ALU.add, ALU.add).then_inc(q_["n2"], 1)
                    dve.wait_ge(q_["gate"], i + 1)
                    dve.wait_ge(q_["n2"], i + 1)
                    for n in range(NCH):
                        dve.tensor_tensor(row[:, 0, chunk(n)], banks[NCH + n][:, :TC], d[:, s, chunk(n)],
                                          ALU.mult).then_inc(q_["gated"], 1)

                dve.sem_inc(q_["gated"], 2 * NCH)
                dve.sem_inc(q_["centred"], START)
                centre(0, 0)
                with dve.Fori(0, KD // 2 - 1) as it:
                    for s in range(2):
                        centre(it * 2 + s + 1, 1 - s)
                        norm(it * 2 + s, s, it)
                centre(KD - 1, 1)
                for s in range(2):
                    norm(KD - 2 + s, s, KD // 2 - 1)


def rwkv_layer(nc, hT, K, cst, vec, A, O, scratch):
    with Stage(nc, "c") as st:
        lora = st.sb("lora", [P, 2, T])
        lora_g2 = st.sb("lora_g2", [G2, T])
        el = st.sb("chunk_decay", [P, KD, NC + NB])
        with Stage(nc, "c1") as s1:
            uT, xx = s1.sb("uT", [P, KD, T]), s1.sb("xx", [P, KD, T])
            rms_norm(nc, "nm1", hT, vec[:, VEC.at["mix"]][:, KD:], uT, K)
            shift_difference(nc, uT, xx, vec, O)
            mixed_projections(nc, uT, xx, vec, lora, lora_g2, A, scratch)
        prepare_chunks(nc, lora, el, K, vec, A, scratch)
        with Stage(nc, "c2") as s2:
            yT = s2.sb("yT", [P, KD, T])
            prompt_chunks(nc, el, yT, K, cst, scratch, O)
            sample_chunk(nc, el, yT, K, cst, A, scratch, O)
            finish_heads(nc, yT, lora, lora_g2, K, vec, A, scratch)
            add_projection(nc, "wo1", lambda k, n: yT[:, k, chunk(n)], KD, A["w_o"], hT)


F32R = mybir.dt.float32r
HALF = T // 2
HC = HALF // 2


def part(half, n):
    return slice(half * HALF + n * HC, half * HALF + (n + 1) * HC)


def local(n):
    return slice(n * HC, (n + 1) * HC)


class SplitDense(Stage):

    def __init__(self, nc, tag, kc):
        super().__init__(nc, tag)
        self.kc = kc

    def __enter__(self):
        super().__enter__()
        self.raw = self.sb("weights", [P, 2, self.kc * P])
        self.hi = self.sb("weights_hi", [P, 2, self.kc * P], F32R)
        self.lo = self.sb("weights_lo", [P, 2, self.kc * P], F32R)
        self.banks = [self.bank(f"out{i}") for i in range(4)]
        self.loaded = [self.sem(f"weights_loaded{s}") for s in range(2)]
        self.hi_ready, self.lo_ready = self.sem("weights_hi_ready"), self.sem("weights_lo_ready")
        self.chunk_done = self.sem("chunk_done")
        self.bank_free = [self.sem(f"bank_free{s}") for s in range(2)]
        return self

    def load(self, sp, source, tiles):
        for s in range(2):
            sp.dma_start(self.raw[:, s], source[s]).then_inc(self.loaded[s], 16)
        with sp.Fori(1, tiles // 2) as it:
            for s in range(2):
                sp.wait_ge(self.lo_ready, it * 2 + s - 1)
                sp.dma_start(self.raw[:, s], source[ds(it * 2 + s, 1)][0]).then_inc(self.loaded[s], 16)

    def split_hi(self, act, it, s):
        act.wait_ge(self.loaded[s], it * 16 + 16)
        act.wait_ge(self.chunk_done, it * 4 + (s + 1) * 2)
        act.activation(self.hi[:, s], self.raw[:, s], ACT.Copy).then_inc(self.hi_ready, 1)

    def split_lo(self, pool, tiles):
        with pool.Fori(0, tiles // 2) as it:
            for s in range(2):
                pool.wait_ge(self.chunk_done, it * 4 + (s + 1) * 2)
                pool.wait_ge(self.hi_ready, it * 2 + s + 1)
                pool.tensor_tensor(self.lo[:, s], self.raw[:, s], self.hi[:, s].bitcast(F32),
                                   ALU.subtract).then_inc(self.lo_ready, 1)

    def multiply(self, pe, hi, lo, tiles, split_parts=None):
        pe.sem_inc(self.chunk_done, 4)
        if split_parts is not None:
            pe.wait_ge(split_parts, KD)
        with pe.Fori(0, tiles // 2) as it:
            for s in range(2):
                pe.wait_ge(self.lo_ready, it * 2 + s + 1)
                for n in range(2):
                    pe.wait_ge(self.bank_free[s], it * 2 + n + 1)
                    out = self.banks[s * 2 + n][:, :HC]
                    for k in range(self.kc):
                        w = slice(k * P, (k + 1) * P)
                        pe.matmul(out, self.hi[:, s, w], hi[:, k, local(n)], start=(k == 0), stop=False)
                        pe.matmul(out, self.hi[:, s, w], lo[:, k, local(n)], start=False, stop=False)
                        last = pe.matmul(out, self.lo[:, s, w], hi[:, k, local(n)], start=False,
                                         stop=(k == self.kc - 1))
                    last.then_inc(self.chunk_done, 1)


def inverse_rms(nc, tag, src, rstd, K):
    with Stage(nc, tag) as st:
        sq = st.sb("squares", [P, 2, T])
        sums = [st.bank(f"sum{n}") for n in range(NCH)]
        squared, summed, mean_ready, inv_ready = (st.sem(n) for n in ("squared", "summed", "mean_ready", "inv_ready"))
        with nc.Block() as block:
            @block.scalar
            def _(act):
                for k in range(KD):
                    if k >= 2:
                        act.wait_ge(summed, k - 1)
                    act.activation(sq[:, k % 2], src[:, k], ACT.Square).then_inc(squared, 1)
                for n in range(NCH):
                    act.wait_ge(inv_ready, n + 1)
                    act.activation(rstd[:, chunk(n)], rstd[:, chunk(n)], ACT.Sqrt)

            @block.tensor
            def _(pe):
                for k in range(KD):
                    pe.wait_ge(squared, k + 1)
                    for n in range(NCH):
                        last = pe.matmul(sums[n][:, :TC], K.ones, sq[:, k % 2, chunk(n)],
                                         start=(k == 0), stop=(k == KD - 1))
                    last.then_inc(summed, 1)

            @block.vector
            def _(dve):
                dve.wait_ge(summed, KD)
                for n in range(NCH):
                    dve.tensor_scalar(rstd[:, chunk(n)], sums[n][:, :TC], 1.0 / D, NORM_EPS,
                                      ALU.mult, ALU.add).then_inc(mean_ready, 1)
                for n in range(NCH):
                    dve.wait_ge(mean_ready, n + 1)
                    dve.reciprocal(rstd[:, chunk(n)], rstd[:, chunk(n)]).then_inc(inv_ready, 1)


def split_gated(nc, tag, hT, half, gain, rstd, uh, ul, source, fh, fl):
    with SplitDense(nc, tag, KD) as st:
        u = st.sb("u", [P, 2, HALF])
        gate, prod = st.sb("gate", [P, 2, HC]), st.sb("product", [P, 2, HC])
        normed, u_hi, u_lo = st.sem("normed"), st.sem("u_hi"), st.sem("u_lo")
        gate_ready, prod_ready, f_hi, f_lo = (st.sem(n) for n in ("gate_ready", "product_ready", "f_hi", "f_lo"))
        cols = slice(half * HALF, (half + 1) * HALF)
        with nc.Block() as block:
            @block.sync
            def _(sp):
                st.load(sp, source, 2 * FT)

            @block.gpsimd
            def _(pool):
                st.split_lo(pool, 2 * FT)

            @block.tensor
            def _(pe):
                st.multiply(pe, uh, ul, 2 * FT, u_lo)

            @block.scalar
            def _(act):
                act.sem_inc(st.bank_free[0], 2)
                for k in range(KD):
                    act.wait_ge(normed, k + 1)
                    act.activation(uh[:, k], u[:, k % 2], ACT.Copy).then_inc(u_hi, 1)
                    if k == 1:
                        st.split_hi(act, 0, 0)

                def tile(it, final):
                    st.split_hi(act, it, 1)
                    for n in range(2):
                        act.wait_ge(st.chunk_done, it * 4 + n + 5)
                        act.wait_ge(prod_ready, it * 2 + n + 1)
                        act.activation(gate[:, n], st.banks[n][:, :HC], ACT.Silu).then_inc(st.bank_free[0], 1)
                        act.wait_ge(st.bank_free[0], it * 2 + n + 3)
                        act.sem_inc(gate_ready, 1)
                    if not final:
                        st.split_hi(act, it + 1, 0)
                    for n in range(2):
                        act.wait_ge(prod_ready, it * 2 + n + 3)
                        act.activation(fh[:, ds(it, 1), local(n)][:, 0], prod[:, n], ACT.Copy).then_inc(f_hi, 1)

                with act.Fori(0, FT - 1) as it:
                    tile(it, False)
                tile(FT - 1, True)

            @block.vector
            def _(dve):
                dve.sem_inc(prod_ready, 2)
                dve.sem_inc(st.bank_free[1], 2)
                dve.sem_inc(f_lo, 2)
                for k in range(KD + 1):
                    if k < KD:
                        if k >= 2:
                            dve.wait_ge(u_lo, k - 1)
                        dve.scalar_tensor_tensor(u[:, k % 2], hT[:, k, cols], gain[:, k:k + 1], rstd[:, cols],
                                                 ALU.mult, ALU.mult).then_inc(normed, 1)
                    if k:
                        dve.wait_ge(u_hi, k)
                        dve.tensor_tensor(ul[:, k - 1], u[:, (k - 1) % 2], uh[:, k - 1].bitcast(F32),
                                          ALU.subtract).then_inc(u_lo, 1)
                with dve.Fori(0, FT) as it:
                    for n in range(2):
                        dve.wait_ge(st.chunk_done, it * 4 + n + 7)
                        dve.wait_ge(gate_ready, it * 2 + n + 1)
                        dve.wait_ge(f_lo, it * 2 + n + 1)
                        dve.tensor_tensor(prod[:, n], st.banks[2 + n][:, :HC], gate[:, n],
                                          ALU.mult).then_inc(st.bank_free[1], 1)
                        dve.wait_ge(st.bank_free[1], it * 2 + n + 3)
                        dve.sem_inc(prod_ready, 1)
                    for n in range(2):
                        dve.wait_ge(f_hi, it * 2 + n + 1)
                        dve.tensor_tensor(fl[:, ds(it, 1), local(n)][:, 0], prod[:, n],
                                          fh[:, ds(it, 1), local(n)][:, 0].bitcast(F32), ALU.subtract).then_inc(f_lo, 1)


def split_add(nc, tag, hi, lo, kc, half, source, hT):
    with SplitDense(nc, tag, kc) as st:
        with nc.Block() as block:
            @block.sync
            def _(sp):
                st.load(sp, source, KD)

            @block.gpsimd
            def _(pool):
                st.split_lo(pool, KD)

            @block.tensor
            def _(pe):
                st.multiply(pe, hi, lo, KD)

            @block.scalar
            def _(act):
                with act.Fori(0, KD // 2) as it:
                    for s in range(2):
                        st.split_hi(act, it, s)

            @block.vector
            def _(dve):
                for s in range(2):
                    dve.sem_inc(st.bank_free[s], 2)
                with dve.Fori(0, KD // 2) as it:
                    for s in range(2):
                        row = hT[:, ds(it * 2 + s, 1)]
                        for n in range(2):
                            dve.wait_ge(st.chunk_done, it * 4 + s * 2 + n + 5)
                            out = row[:, 0, part(half, n)]
                            dve.tensor_tensor(out, st.banks[s * 2 + n][:, :HC], out, ALU.add).then_inc(st.bank_free[s], 1)


def ffn_layer(nc, hT, l, K, vec, A):
    with Stage(nc, f"f{l}") as st:
        rstd = st.sb("rstd", [P, T])
        inverse_rms(nc, f"nf{l}", hT, rstd, K)
        fh, fl = st.sb("inner_hi", [P, FT, HALF], F32R), st.sb("inner_lo", [P, FT, HALF], F32R)
        gain = vec[:, VEC.at["ffn"]][:, l * KD:(l + 1) * KD]
        for half in range(2):
            with Stage(nc, f"f{l}u{half}") as s2:
                uh, ul = s2.sb("u_hi", [P, KD, HALF], F32R), s2.sb("u_lo", [P, KD, HALF], F32R)
                split_gated(nc, f"gu{l}{half}", hT, half, gain, rstd, uh, ul, A[f"w_gu{l}"], fh, fl)
            split_add(nc, f"dn{l}{half}", fh, fl, FT, half, A[f"w_down{l}"], hT)


def program(nc, A, O):
    Stage.finished = []
    scratch = scratch_buffers(nc)
    with Stage(nc, "all") as st:
        hT = st.sb("hT", [P, KD, T])
        cst, vec = st.sb("constants", [P, CONST.n]), st.sb("vectors", [P, VEC.n])
        K = Constants(cst)
        store_or_load(nc, "in", [(hT[:], A["x"]), (cst[:], A["cst"]), (vec[:], A["vec"])])
        attention_layer(nc, hT, K, cst, vec, A, O)
        ffn_layer(nc, hT, 0, K, vec, A)
        rwkv_layer(nc, hT, K, cst, vec, A, O, scratch)
        ffn_layer(nc, hT, 1, K, vec, A)
        yT = st.sb("yT", [P, KD, T])
        rms_norm(nc, "nfin", hT, vec[:, VEC.at["final"]], yT, K)
        store_or_load(nc, "out", [(O["y"], yT[:])])


OUTPUTS = {
    "y": (P, KD, T), "k": (P, AH, T), "v": (P, AH, T), "conv_p": (P, BT, LEAD), "conv_s": (P, BT, NB, LEAD),
    "shift": (P, KD, 1 + NB), "wkv_p": (P, PAIRS, DH), "wkv_s": (PAIRS, P, NB, DH),
}


def kernel(**inputs):
    import concourse.bacc as bacc
    from concourse.bass_utils import run_bass_kernel_spmd

    nc = bacc.Bacc("TRN2", target_bir_lowering=False, num_devices=1)
    arrays = {"in_" + n: np.ascontiguousarray(a) for n, a in lay_out(inputs).items()}
    A = {n[3:]: nc.dram_tensor(n, a.shape, mybir.dt.from_np(a.dtype), kind="ExternalInput").ap()
         for n, a in arrays.items()}
    O = {n: nc.dram_tensor("out_" + n, s, F32, kind="ExternalOutput").ap() for n, s in OUTPUTS.items()}
    program(nc, A, O)
    r = run_bass_kernel_spmd(nc, [arrays], core_ids=[0]).results[0]
    out = {n: np.asarray(r["out_" + n]) for n in OUTPUTS}

    def tokens(x):
        return np.ascontiguousarray(x.transpose(2, 1, 0)).reshape(x.shape[2], -1)

    y, k, v, shift = (tokens(out[n]) for n in ("y", "k", "v", "shift"))
    heads = (AH, 2 * DH)
    conv_s = out["conv_s"].transpose(2, 3, 1, 0).reshape(1, NB, LEAD, BT * P)
    wkv_p = out["wkv_p"].reshape(2, DH, PAIRS, DH).transpose(2, 0, 3, 1).reshape(1, 1, 2 * PAIRS, DH, DH)
    wkv_s = out["wkv_s"].reshape(PAIRS, 2, DH, NB, DH).transpose(3, 0, 1, 4, 2).reshape(1, NB, 2 * PAIRS, DH, DH)
    got = (
        y[:TP].reshape(1, TP, D), y[TP:].reshape(NB, NT, D),
        k[:TP].reshape(1, 1, TP, *heads), v[:TP].reshape(1, 1, TP, *heads),
        tokens(out["conv_p"]).reshape(1, 1, LEAD, BT * P), wkv_p, shift[:1].reshape(1, 1, D),
        k[TP:].reshape(1, NB, NT, *heads), v[TP:].reshape(1, NB, NT, *heads),
        conv_s, wkv_s, shift[1:].reshape(1, NB, D),
    )
    return tuple(np.ascontiguousarray(g) for g in got)
```
